# Optimizing a Trainium2 kernel written in Bass

```python
import math
import jax, jax.numpy as jnp
from jax import lax
import numpy as np

D_MODEL = 1024
BATCH = 1
SEQ = 512
DEPTH = 4
DEC_BATCH = 8
DEC_SEQ = 1
PAST_LEN = 512
PAGE_SIZE = 128

N_MIXERS = 3
N_RET_LAYERS = (DEPTH + 2) // 3
N_POOL_LAYERS = (DEPTH + 1) // 3
N_DSA_LAYERS = DEPTH // 3
RET_HEADS = 4
RET_KEY_DIM = D_MODEL // RET_HEADS
RET_VAL_DIM = 2 * RET_KEY_DIM
RET_CHUNK = 128
RET_IN = 2 * RET_HEADS * RET_KEY_DIM + 2 * RET_HEADS * RET_VAL_DIM
POOL_WINDOWS = (2, 4, 8, 16)
POOL_GROUP_DIM = D_MODEL // len(POOL_WINDOWS)
POOL_HIST = max(POOL_WINDOWS) - 1
ATTN_HEADS = 8
ATTN_HEAD_DIM = D_MODEL // ATTN_HEADS
IDX_HEADS = 4
IDX_DIM = 64
IDX_SCALE = (IDX_HEADS ** -0.5) * (IDX_DIM ** -0.5)
TOPK_MAX = 256
DSA_Q_BLOCK = 16
DSA_IN = 3 * D_MODEL + IDX_HEADS * IDX_DIM + IDX_DIM + IDX_HEADS
FFN_DIM = -(-8 * D_MODEL // (3 * 256)) * 256
ROPE_THETA = 10000.0
LN_EPS = 1e-5
DEEPNORM_ALPHA = (2.0 * DEPTH) ** 0.25
DEEPNORM_BETA = (8.0 * DEPTH) ** -0.25

kernel_name = "hybrid_retention_pool_dsa_decoder_step"

F32 = jnp.float32

def rope(x, pos):
    half = x.shape[-1] // 2
    inv = jnp.power(ROPE_THETA, -jnp.arange(half, dtype=F32) / half)
    ang = pos.astype(F32)[:, None] * inv[None, :]
    cos = jnp.cos(ang)[None, :, None, :]
    sin = jnp.sin(ang)[None, :, None, :]
    xf = x.astype(F32)
    x1, x2 = xf[..., :half], xf[..., half:]
    return jnp.concatenate([x1 * cos - x2 * sin, x2 * cos + x1 * sin], axis=-1).astype(x.dtype)

def layer_norm(x, g, b):
    xf = x.astype(F32)
    mu = jnp.mean(xf, axis=-1, keepdims=True)
    var = jnp.mean(jnp.square(xf - mu), axis=-1, keepdims=True)
    return ((xf - mu) * lax.rsqrt(var + LN_EPS) * g.astype(F32) + b.astype(F32)).astype(x.dtype)

def deepnorm_residual(x, h, g, b):
    return layer_norm(DEEPNORM_ALPHA * x + h, g, b)

def swiglu(x, w_in, w_out):
    a, u = jnp.split(x @ w_in, 2, axis=-1)
    return (jax.nn.silu(a) * u) @ w_out

def retention_chunked(q, k, v, s0):
    b, l, h, _ = q.shape
    c = math.gcd(l, RET_CHUNK)
    n = l // c
    lg = jnp.log1p(-jnp.exp2(-5.0 - jnp.arange(h, dtype=F32)))
    i = jnp.arange(c, dtype=F32)
    diff = i[:, None] - i[None, :]
    decay_in = jnp.where(diff[None] >= 0, jnp.exp(jnp.maximum(diff, 0.0)[None] * lg[:, None, None]), 0.0)
    q_dec = jnp.exp((i[None, :] + 1.0) * lg[:, None]).T[None, :, :, None]
    k_dec = jnp.exp((c - 1.0 - i[None, :]) * lg[:, None]).T[None, :, :, None]
    c_dec = jnp.exp(c * lg)[None, :, None, None]

    def to_chunks(a):
        return a.reshape(b, n, c, *a.shape[2:]).swapaxes(0, 1)

    def step(s, blk):
        qc, kc, vc = blk
        att = jnp.einsum('bihd,bjhd->bhij', qc, kc) * decay_in
        inner = jnp.einsum('bhij,bjhe->bihe', att, vc)
        cross = jnp.einsum('bihd,bhde->bihe', qc * q_dec, s)
        s_new = s * c_dec + jnp.einsum('bjhd,bjhe->bhde', kc * k_dec, vc)
        return s_new, inner + cross

    s_fin, o = lax.scan(step, s0, (to_chunks(q), to_chunks(k), to_chunks(v)))
    return o.swapaxes(0, 1).reshape(b, l, h, -1), s_fin

def retention_mixer(x, s0, pos, w_in, norm_g, w_out):
    b, l, _ = x.shape
    hk = RET_HEADS * RET_KEY_DIM
    hv = RET_HEADS * RET_VAL_DIM
    q, k, v, g = jnp.split(x @ w_in, [hk, 2 * hk, 2 * hk + hv], axis=-1)
    q = rope(q.reshape(b, l, RET_HEADS, RET_KEY_DIM), pos).astype(F32)
    k = rope(k.reshape(b, l, RET_HEADS, RET_KEY_DIM), pos).astype(F32) * (RET_KEY_DIM ** -0.5)
    v = v.reshape(b, l, RET_HEADS, RET_VAL_DIM).astype(F32)
    o, s_fin = retention_chunked(q, k, v, s0.astype(F32))
    mu = jnp.mean(o, axis=-1, keepdims=True)
    var = jnp.mean(jnp.square(o - mu), axis=-1, keepdims=True)
    o = ((o - mu) * lax.rsqrt(var + LN_EPS)).reshape(b, l, hv) * norm_g.astype(F32)
    y = (jax.nn.silu(g.astype(F32)) * o).astype(x.dtype) @ w_out
    return y, s_fin

def pool_mixer(x_hist, x_new, pos0, w_grp, scale):
    l = x_new.shape[1]
    x_ext = jnp.concatenate([x_hist.astype(x_new.dtype), x_new], axis=1)
    xf = x_ext.astype(F32)
    cs = jnp.pad(jnp.cumsum(xf, axis=1), ((0, 0), (1, 0), (0, 0)))
    pos = pos0 + jnp.arange(l)
    outs = []
    for gi, w in enumerate(POOL_WINDOWS):
        lo, hi = gi * POOL_GROUP_DIM, (gi + 1) * POOL_GROUP_DIM
        wsum = cs[:, POOL_HIST + 1:POOL_HIST + 1 + l, lo:hi] - cs[:, POOL_HIST + 1 - w:POOL_HIST + 1 - w + l, lo:hi]
        cnt = jnp.minimum(w, pos + 1).astype(F32)
        d = wsum / cnt[None, :, None] - xf[:, POOL_HIST:, lo:hi]
        outs.append(jnp.einsum('bld,de->ble', d, w_grp[gi].astype(F32)))
    y = (jnp.concatenate(outs, axis=-1) * scale.astype(F32)).astype(x_new.dtype)
    return y, x_ext[:, -POOL_HIST:]

def dsa_project(x, pos, w_in):
    b, l, _ = x.shape
    d = D_MODEL
    q, k, v, qi, ki, wi = jnp.split(
        x @ w_in, [d, 2 * d, 3 * d, 3 * d + IDX_HEADS * IDX_DIM, 3 * d + IDX_HEADS * IDX_DIM + IDX_DIM], axis=-1)
    q = rope(q.reshape(b, l, ATTN_HEADS, ATTN_HEAD_DIM), pos)
    k = rope(k.reshape(b, l, ATTN_HEADS, ATTN_HEAD_DIM), pos)
    v = v.reshape(b, l, ATTN_HEADS, ATTN_HEAD_DIM)
    qi = rope(qi.reshape(b, l, IDX_HEADS, IDX_DIM), pos)
    ki = rope(ki.reshape(b, l, 1, IDX_DIM), pos)[:, :, 0, :]
    return q, k, v, qi, ki, wi

def indexer_topk(qi, wi, ki_all, pos_q, n_top):
    rel = jax.nn.relu(jnp.einsum('bqhd,bkd->bqhk', qi.astype(F32), ki_all.astype(F32)))
    score = jnp.einsum('bqh,bqhk->bqk', wi.astype(F32) * IDX_SCALE, rel)
    visible = jnp.arange(ki_all.shape[1])[None, :] <= pos_q[:, None]
    score = jnp.where(visible[None], score, -jnp.inf)
    _, idx = lax.top_k(score, n_top)
    valid = idx <= pos_q[None, :, None]
    return idx, valid

def sparse_attend(q, k_sel, v_sel, valid):
    s = jnp.einsum('bqhd,bqkhd->bqhk', q.astype(F32), k_sel.astype(F32)) * (ATTN_HEAD_DIM ** -0.5)
    s = jnp.where(valid[:, :, None, :], s, -jnp.inf)
    p = jax.nn.softmax(s, axis=-1)
    return jnp.einsum('bqhk,bqkhd->bqhd', p, v_sel.astype(F32)).astype(q.dtype)

_gather_rows = jax.vmap(lambda rows, ix: rows[ix])

def dsa_prompt(x, w_in, w_out):
    b, l, _ = x.shape
    pos = jnp.arange(l)
    q, k, v, qi, ki, wi = dsa_project(x, pos, w_in)
    n_top = min(TOPK_MAX, l // 4)
    nb = l // DSA_Q_BLOCK

    def blockify(a):
        return a.reshape(b, nb, DSA_Q_BLOCK, *a.shape[2:]).swapaxes(0, 1)

    def block(args):
        qb, qib, wib, posb = args
        idx, valid = indexer_topk(qib, wib, ki, posb, n_top)
        return sparse_attend(qb, _gather_rows(k, idx), _gather_rows(v, idx), valid)

    o = lax.map(block, (blockify(q), blockify(qi), blockify(wi), pos.reshape(nb, DSA_Q_BLOCK)))
    o = o.swapaxes(0, 1).reshape(b, l, ATTN_HEADS * ATTN_HEAD_DIM)
    return o @ w_out, k, v, ki

def dsa_sample(x, cache_k, cache_v, cache_kidx, page_table, w_in, w_out):
    b, l, _ = x.shape
    pos = PAST_LEN + jnp.arange(l)
    q, k, v, qi, ki, wi = dsa_project(x, pos, w_in)
    ki_past = cache_kidx[page_table].reshape(b, PAST_LEN, IDX_DIM)
    ki_all = jnp.concatenate([ki_past.astype(ki.dtype), ki], axis=1)
    n_top = min(TOPK_MAX, (PAST_LEN + l) // 4)
    idx, valid = indexer_topk(qi, wi, ki_all, pos, n_top)
    from_past = idx < PAST_LEN
    pidx = jnp.minimum(idx, PAST_LEN - 1)
    phys = _gather_rows(page_table, pidx // PAGE_SIZE)
    off = pidx % PAGE_SIZE
    nidx = jnp.clip(idx - PAST_LEN, 0, l - 1)
    sel = from_past[..., None, None]
    k_sel = jnp.where(sel, cache_k[phys, off], _gather_rows(k, nidx))
    v_sel = jnp.where(sel, cache_v[phys, off], _gather_rows(v, nidx))
    o = sparse_attend(q, k_sel, v_sel, valid).reshape(b, l, ATTN_HEADS * ATTN_HEAD_DIM)
    return o @ w_out, k, v, ki

def setup_inputs(seed: int = 0) -> dict:
    key = jax.random.key(seed)
    ks = jax.random.split(key, 24)
    n_pages = PAST_LEN // PAGE_SIZE
    n_used = DEC_BATCH * n_pages
    n_phys = n_used + (n_used + 3) // 4

    def nrm(k, shape, scale):
        return jax.random.normal(k, shape, F32) * scale

    hv = RET_HEADS * RET_VAL_DIM
    return {
        "x_prompt": nrm(ks[0], (BATCH, SEQ, D_MODEL), 1.0),
        "x_sample": nrm(ks[1], (DEC_BATCH, DEC_SEQ, D_MODEL), 1.0),
        "state_ret": nrm(ks[2], (N_RET_LAYERS, DEC_BATCH, RET_HEADS, RET_KEY_DIM, RET_VAL_DIM), 0.5),
        "state_pool": nrm(ks[3], (N_POOL_LAYERS, DEC_BATCH, POOL_HIST, D_MODEL), 1.0),
        "cache_k": nrm(ks[4], (N_DSA_LAYERS, n_phys, PAGE_SIZE, ATTN_HEADS, ATTN_HEAD_DIM), 1.0),
        "cache_v": nrm(ks[5], (N_DSA_LAYERS, n_phys, PAGE_SIZE, ATTN_HEADS, ATTN_HEAD_DIM), 1.0),
        "cache_kidx": nrm(ks[6], (N_DSA_LAYERS, n_phys, PAGE_SIZE, IDX_DIM), 1.0),
        "page_table": jax.random.permutation(ks[7], n_phys)[:n_used].reshape(DEC_BATCH, n_pages).astype(jnp.int32),
        "ret_w_in": nrm(ks[8], (N_RET_LAYERS, D_MODEL, RET_IN), D_MODEL ** -0.5),
        "ret_norm_g": 1.0 + nrm(ks[9], (N_RET_LAYERS, hv), 0.02),
        "ret_w_out": nrm(ks[10], (N_RET_LAYERS, hv, D_MODEL), hv ** -0.5 * DEEPNORM_BETA),
        "pool_w_grp": nrm(ks[11], (N_POOL_LAYERS, len(POOL_WINDOWS), POOL_GROUP_DIM, POOL_GROUP_DIM),
                          POOL_GROUP_DIM ** -0.5 * DEEPNORM_BETA),
        "pool_scale": 1.0 + nrm(ks[12], (N_POOL_LAYERS, D_MODEL), 0.02),
        "dsa_w_in": nrm(ks[13], (N_DSA_LAYERS, D_MODEL, DSA_IN), D_MODEL ** -0.5),
        "dsa_w_out": nrm(ks[14], (N_DSA_LAYERS, D_MODEL, D_MODEL), D_MODEL ** -0.5 * DEEPNORM_BETA),
        "ffn_w_in": nrm(ks[15], (DEPTH, D_MODEL, 2 * FFN_DIM), D_MODEL ** -0.5),
        "ffn_w_out": nrm(ks[16], (DEPTH, FFN_DIM, D_MODEL), FFN_DIM ** -0.5 * DEEPNORM_BETA),
        "ln_g": 1.0 + nrm(ks[17], (DEPTH, 2, D_MODEL), 0.02),
        "ln_b": nrm(ks[18], (DEPTH, 2, D_MODEL), 0.02),
    }

def reference(x_prompt, x_sample, state_ret, state_pool, cache_k, cache_v, cache_kidx, page_table,
              ret_w_in, ret_norm_g, ret_w_out, pool_w_grp, pool_scale, dsa_w_in, dsa_w_out,
              ffn_w_in, ffn_w_out, ln_g, ln_b):
    xp, xs = x_prompt, x_sample
    bp, lp, _ = xp.shape
    ls = xs.shape[1]
    pos_p = jnp.arange(lp)
    pos_s = PAST_LEN + jnp.arange(ls)
    ret_p, ret_s, pool_p, pool_s = [], [], [], []
    kp_l, vp_l, kip_l, ks_l, vs_l, kis_l = [], [], [], [], [], []
    for i in range(DEPTH):
        kind, j = i % N_MIXERS, i // N_MIXERS
        if kind == 0:
            s_zero = jnp.zeros((bp, RET_HEADS, RET_KEY_DIM, RET_VAL_DIM), F32)
            hp, sp = retention_mixer(xp, s_zero, pos_p, ret_w_in[j], ret_norm_g[j], ret_w_out[j])
            hs, ss = retention_mixer(xs, state_ret[j], pos_s, ret_w_in[j], ret_norm_g[j], ret_w_out[j])
            ret_p.append(sp)
            ret_s.append(ss)
        elif kind == 1:
            hist0 = jnp.zeros((bp, POOL_HIST, D_MODEL), xp.dtype)
            hp, sp = pool_mixer(hist0, xp, 0, pool_w_grp[j], pool_scale[j])
            hs, ss = pool_mixer(state_pool[j], xs, PAST_LEN, pool_w_grp[j], pool_scale[j])
            pool_p.append(sp)
            pool_s.append(ss)
        else:
            hp, kp, vp, kip = dsa_prompt(xp, dsa_w_in[j], dsa_w_out[j])
            hs, kss, vss, kis = dsa_sample(xs, cache_k[j], cache_v[j], cache_kidx[j], page_table,
                                           dsa_w_in[j], dsa_w_out[j])
            kp_l.append(kp)
            vp_l.append(vp)
            kip_l.append(kip)
            ks_l.append(kss)
            vs_l.append(vss)
            kis_l.append(kis)
        xp = deepnorm_residual(xp, hp, ln_g[i, 0], ln_b[i, 0])
        xs = deepnorm_residual(xs, hs, ln_g[i, 0], ln_b[i, 0])
        xp = deepnorm_residual(xp, swiglu(xp, ffn_w_in[i], ffn_w_out[i]), ln_g[i, 1], ln_b[i, 1])
        xs = deepnorm_residual(xs, swiglu(xs, ffn_w_in[i], ffn_w_out[i]), ln_g[i, 1], ln_b[i, 1])
    return (xp, xs, jnp.stack(ret_p), jnp.stack(ret_s), jnp.stack(pool_p), jnp.stack(pool_s),
            jnp.stack(kp_l), jnp.stack(vp_l), jnp.stack(kip_l), jnp.stack(ks_l), jnp.stack(vs_l), jnp.stack(kis_l))


_drawn_inputs = setup_inputs


def setup_inputs(seed=0):
    import zlib

    import numpy as np

    out = dict(_drawn_inputs(seed))
    spreads = {}
    factors = {'ret_norm_g': 8.0, 'pool_scale': 8.0}
    for name, (base, spread) in spreads.items():
        noise = np.random.default_rng([zlib.crc32(name.encode()), seed]).standard_normal(out[name].shape)
        drawn = base * np.exp(spread * noise) if base else spread * noise
        out[name] = __import__('jax').numpy.asarray(drawn.astype(out[name].dtype))
    for name, factor in factors.items():
        out[name] = (out[name] * factor).astype(out[name].dtype)
    return out
```

```python
from contextlib import ExitStack

import numpy as np

import concourse.bass as bass
from concourse import mybir

P = 128
D = 1024
DC = D // P
SEQ = 512
NB = 8
T = SEQ + NB
HALF = T // 2
QT = SEQ // P
DEPTH = 4
ALPHA = (2.0 * DEPTH) ** 0.25
EPS = 1e-5
RH, RK, RV = 4, 256, 512
KC, VC = RK // P, RV // P
WINDOWS = (2, 4, 8, 16)
HIST = 15
AH, AD = 8, 128
IH, ID = 4, 64
TOPK = 128
F = 2816
FA, FB = 12, 10
PAGES, NPHYS = 4, 40
PAST = 512
SLOT = 12 * P
BIG = 1.0e30
GONE = -3.0e38
ASCALE = float(AD) ** -0.5
ISCALE = (IH ** -0.5) * (ID ** -0.5)

ALU = mybir.AluOpType
ACT = mybir.ActivationFunctionType
AX = mybir.AxisListType
F32 = mybir.dt.float32
F32R = mybir.dt.float32r
I32 = mybir.dt.int32

STAGES = [("start", 1, 0)]
for _l, _kind in enumerate(("ret", "pool", "dsa", "ret")):
    if _kind == "ret":
        STAGES += [(f"ret{_l}", RH, 20), (f"sums{_l}", 1, 0)]
    elif _kind == "pool":
        STAGES += [(f"pool{_l}", 1, 4)]
    else:
        STAGES += [(f"idx{_l}", 1, 4), (f"q{_l}", 1, 8), (f"kv{_l}", AH // 2, 4), (f"past{_l}", 1, 0), (f"proj{_l}", 1, 8)]
    STAGES += [(f"norm{_l}a", 1, 0), (f"up{_l}a", FA // 2, 4), (f"down{_l}a", 1, 8),
               (f"up{_l}b", FB // 2, 4), (f"down{_l}b", 1, 8), (f"norm{_l}b", 1, 0)]
STAGES += [("end", 1, 0)]

RET = dict(
    raw_qk=4, raw_v=4, sil_g=4, qk_hi=2, kn_hi=4, v_hi=5, att_hi=4, st_sc=8, sf_cp=2, gate_hi=5,
    rope=8, qs=1, qk_lo=2, kn_lo=4, v_lo=5, att_m=4, att_lo=4, sg_n=4, s_new=16, o_bn=5, o_ag=5, o_n=5,
    gate_m=5, gate_lo=5, z_add=8, sn_cp=1,
    rs_e=5, rs_p=5, kt=2, vt=5, att=4, o_mm=4, vb=8, so_mm=8, sf_mm=2, ot=5,
    head_in=48, sf_out=32, st_in0=32, st_in1=32, st_in2=32, st_in3=32,
    st_out0=32, st_out1=32, st_out2=32, st_out3=32, xs=0)
NORM = dict(stat=4, ln_m=1, ln_v=3, ln_sd=1, ln_rs=1, ln_d=8, ln_e=8, x_n=8, x_hi=8, x_lo=8)
HEAD_START = dict(z_add=8, h_lo=2, sil=1, h_raw=1, d_rope=3, o_lo=1, p_lo=1, pv=1, vv_tp=1,
                  kr_a=4, kr_v=4)
PER = {
    "start": dict(x_tp=8, xs_tp=8, x_t=16, x_hi=8, x_lo=8, x_in=48, const=16 * 3, pages_in=16, tiny_c=2, carried=0, idr=1, **HEAD_START,
                  w_hi=0, w_lo=0, mm=0, w_in0=0, w_in1=0, w_in2=0, w_in3=0),
    "ret": RET,
    "up_a": dict(sil=2, h_raw=2, h_hi=2, h_lo=2), "up_b": dict(sil=2, h_raw=2, h_hi=2, h_lo=2),
    "down_a": dict(z_add=8), "down_b": dict(z_add=8, sq=8, sum_s=8, sum_q=8),
    "sums": dict(sq=8, sum_s=8, sum_q=8),
    "norm": NORM,
    "pool": dict(pl_in=16 * 3, pl_tail=2, pl_hist=2, pl_out=16 * 3, tail_cp=2, win=48, d_hi=4, d_lo=4, y_sc=8,
                 z_add=8, sq=8, sum_s=8, sum_q=8),
    "idx": dict(tab_in=16 * 5, kv_out=32, d_raw=4, rot=3, d_rope=9, d_hi=3, d_lo=3, wi_tp=1,
                ki_cp=4, s_idx=12, rl=12, sc=15, sv_i=3),
    "q": dict(pick=96, bias=4, d_raw=8, rot=8, d_rope=24, q_hi=8, q_lo=8, qs_cp=8),
    "kv": dict(d_raw=4, rot=2, d_rope=6, qa_h=2, qa_l=2, k_hi=2, k_lo=2, ks_cp=4, kk_tp=2, vv_tp=2, kn_cp=4, vn_cp=4,
               vv_hi=2, vv_lo=2, kv_out=128, s_mm=8, s_sc=8, nmx=8, p_exp=8, p_rc=8, p_n=8, p_tp=8, p_hi=8, p_lo=8,
               pv=2, o_hi=2, o_lo=2),
    "past": dict(pt_in=16 * 3, kx_in=16 * 32, qi_t=2, qi_c=2, qm=13, prodi=1, ki_w=1, wcol=1, kx_t=8, kx_c=8, kx_mm=1, rel=2,
                 lw=1, sc_mm=1, sc_cp=2, sp_pick=33, b64_mm=1, b64=2, kp_in0=64 * 8, kp_in1=64 * 8, qc=8,
                 kr_a=16, kr_v=16, kmm=32, pz=1, s64=1, pr=1, sm=2, smx=2, sm_e=1, sm_n=2,
                 pt_t=1, dg=1, pc=8, ov=8, om=1, oh=1, osum=2, o_hi=1, o_lo=1),
    "proj": dict(z_add=8, sq=8, sum_s=8, sum_q=8),
    "end": dict(y_tp=8, ys_tp=8, y_cp=16, y_out=32),
}


SHARED = dict(ki_w="qs", wcol="att", kx_t="att_m", kx_c="att_hi", kx_mm="att_lo", rel="gate_hi", lw="gate_lo",
              sc_mm="gate_m", sc_cp="kn_hi", b64_mm="sf_cp", b64="kt", qi_t="o_ag", qi_c="o_bn", qm="o_mm",
              prodi="o_n", pt_t="ot", om="qk_hi", oh="kn_lo", dg="qk_lo", ov="rope", osum="s_new", sm_e="sg_n", sm_n="sil_g",
              smx="raw_qk", sm="so_mm", pr="st_sc", s64="v_hi")


def kind_of(stage):
    name = "".join(ch for ch in stage if not ch.isdigit())
    if name.startswith("norm"):
        return "norm"
    if name[:-1] in ("up", "down"):
        return name[:-1] + "_" + name[-1]
    return name


class Marks:

    def __init__(self, nc, ctx):
        names = sorted({n for per in PER.values() for n in per} - set(SHARED))
        self.sem = {n: ctx.enter_context(nc.semaphore(n)) for n in names}
        self.sem.update({n: self.sem[by] for n, by in SHARED.items()})
        self.first, self.unit0, self.where = {}, {}, {}
        count, unit = dict.fromkeys(names, 0), 0
        for stage, passes, units in STAGES:
            self.first[stage], self.unit0[stage] = dict(count), unit
            self.where[stage] = (passes, units)
            unit += passes * units
            for n, per in self.per(stage).items():
                count[n] += passes * per
        self.units = unit
        self.total = count

    def per(self, stage):
        return {SHARED.get(n, n): per for n, per in PER[kind_of(stage)].items()}

    def here(self, stage, i=0):
        per, first = self.per(stage), self.first[stage]

        def at(name, k):
            name = SHARED.get(name, name)
            return self.sem[name], i * per.get(name, 0) + (first[name] + k)
        return at

    def unit(self, stage, i, k):
        return i * self.where[stage][1] + (self.unit0[stage] + k)

    def next_unit(self, stage, i, k):
        passes, units = self.where[stage]
        names = [s for s, _, u in STAGES if u]
        while k >= units:
            if isinstance(i, int) and i == passes - 1:
                at = names.index(stage) + 1
                if at == len(names):
                    return None
                k -= units
                stage, i = names[at], 0
                passes, units = self.where[stage]
            else:
                k -= units
                i = i + 1
        return stage, i, k


def passes(eng, n, first=0):
    if first:
        yield 0
    if n > 1:
        with eng.Fori(first, n - 1) as i:
            yield i
    yield n - 1


POOL_OPS = [9, 20, 33, 48]
SC_AT = [0, 0, 2 * P, 5 * P]
BIAS_AT = [0, P, 3 * P, 6 * P]


def sums(stage):
    return "sums" + stage[3:]


def prompt_halves():
    return [slice(0, HALF), slice(HALF, T)]


ATT_AT = [0, 512, 896, 1152]
VT_BANK, AT_BANK, O_BANK, SF_BANK = [6, 7, 4, 5, 4], [4, 5, 6, 7], [5, 4, 5, 4, 6], [5, 4]
OT_BANK = [5, 4, 5, 4, 7]


def trunk(nc, A, O):
    with ExitStack() as ctx:
        marks = Marks(nc, ctx)
        S = marks.sem
        V, C, G, M = nc.vector, nc.scalar, nc.gpsimd, nc.tensor

        def sb(name, shape, dt=F32):
            return ctx.enter_context(nc.sbuf_tensor(name, shape, dt))

        x = sb("x", [P, DC, T])
        x_h = sb("x_h", [P, DC, T], F32R)
        x_l = sb("x_l", [P, DC, T], F32R)
        w_raw = sb("w_raw", [P, 4, SLOT])
        w_h = sb("w_h", [P, 2, SLOT], F32R)
        w_l = sb("w_l", [P, 2, SLOT], F32R)
        rr = sb("rr", [P, 13984], F32R)
        wf = sb("wf", [P, 11924])
        rtab = sb("rtab", [P, 2, T])
        ident = sb("ident", [P, P])
        ident_r = sb("ident_r", [P, P], F32R)
        avg = sb("avg", [P, P])
        lncol = sb("lncol", [P, 2, DEPTH * 2 * DC])
        headc = sb("headc", [P, 16])
        tiny = sb("tiny", [P, 192])
        pages = sb("pages", [1, NB * PAGES], I32)
        ps = ctx.enter_context(nc.psum_tensor("ps", [P, 8, 512], F32))

        def view(buf, start, a, b):
            return buf[:, start:start + a * b].rearrange("p (a b) -> p a b", a=a)

        h_h, h_l = view(rr, 0, FA, T), view(rr, FA * T, FA, T)
        sil, h_raw = view(wf, 4160, 2, T), view(wf, 5200, 2, T)
        sum_s, sum_q, ln_m, ln_r = (wf[:, n * T:(n + 1) * T] for n in range(4))
        sq, ln_e = view(wf, 2080, 2, T), view(wf, 2080, DC, T)
        qk_h, qk_l = view(rr, 0, 4, T), view(rr, 2080, 4, T)
        kn_h, kn_l = view(rr, 4160, QT, RK), view(rr, 5184, QT, RK)
        v_h, v_l = view(rr, 6208, QT + 1, RV), view(rr, 8768, QT + 1, RV)
        att_h, att_l = rr[:, 11328:12608], rr[:, 12608:13888]
        gate_h, gate_l = qk_h, qk_l
        raw, q_f, k_f, sg = view(wf, 0, 4, T), view(wf, 2080, 2, T), view(wf, 3120, 2, T), view(wf, 4160, 4, T)
        mask = wf[:, 6240:6752]
        st = wf[:, 6752:10848].rearrange("p (r d e) -> p r d e", r=4, d=KC)
        sf = view(wf, 10900, KC, RV)
        am = q_f

        def normed(t):
            return raw[:, t, 0:RV] if t < QT else q_f[:, 0, 0:RV]
        qz = tiny[:, 64:192].rearrange("p (d b n) -> p d b n", d=KC, b=NB)
        bn = tiny[:, 0:30].rearrange("p (t s) -> p t s", t=5)
        mv = tiny[:, 30:40].rearrange("p (t s) -> p t s", t=5)
        ve, rs, mhalf = tiny[:, 40:45], tiny[:, 45:50], tiny[:, 50:51]
        hist, inv, tail = wf[:, 6240:7264], wf[:, 7264:7328], wf[:, 7328:8352]
        win = [view(wf, 8352, 2, SEQ), view(wf, 9376, 2, SEQ)]
        dd, ysc = view(wf, 10400, 2, T), view(wf, 4160, 2, T)
        d_h, d_l = view(rr, 0, DC, T), view(rr, DC * T, DC, T)
        d_raw, d_f, d_t = view(wf, 0, 2, T), view(wf, 1040, 2, T), wf[:, 2080:2600]
        rl = view(wf, 2600, 2, SEQ)
        kn, vn = view(wf, 2600, QT, P), view(wf, 3112, QT, P)
        pe_ = view(wf, 3624, 2, SEQ)
        dtab, itab = view(wf, 6240, 2, T), view(wf, 7280, 2, T)
        bias, sc = wf[:, 8320:9600], wf[:, 9600:10752]
        rotm, roti, causal = wf[:, 10752:10880], wf[:, 10880:11008], wf[:, 11008:11136]
        kvs = wf[:, 11136:11392].rearrange("p (w d) -> p w d", w=2)
        qs_d, ks_d, vs_d = (wf[:, 11392 + 64 * n:11456 + 64 * n].rearrange("p (h b) -> p h b", h=AH) for n in range(3))
        qi_h, qi_l = view(rr, 8320, 2, T), view(rr, 9360, 2, T)
        ki_h, ki_l = rr[:, 10400:10920], rr[:, 10920:11440]
        q_h, q_l = view(rr, 0, AH, T), view(rr, AH * T, AH, T)
        qa_h, qa_l, ka_h, ka_l = (rr[:, 8320 + n * T:8840 + n * T] for n in range(4))
        va_h, va_l = view(rr, 10400, QT, P), view(rr, 10912, QT, P)
        p_h, p_l = view(rr, 11424, 2, SEQ), view(rr, 12448, 2, SEQ)
        o_h, o_l = q_h, q_l
        kix_n, kix_s = view(wf, 3624, QT, ID), wf[0:NB, 3880:3944]
        qi_d, ki_d = view(wf, 11584, 2, NB), wf[:, 11600:11608]
        mx8, wi = tiny[:, 0:8], tiny[:, 8:24].rearrange("p (t h) -> p t h", t=QT)
        wi_s = tiny[:, 24:28]
        dmx, dnm, dsm, drc = (tiny[:, 32 + 4 * n:36 + 4 * n] for n in range(4))
        kvp = wf[:, 0:8192].rearrange("p (s j e) -> p s j e", s=2, j=PAGES)
        kix = view(wf, 8192, NB * PAGES, ID)
        pz = wf[:, 8192:10240].rearrange("p (j b n) -> p j b n", j=PAGES, b=NB)
        om, pick_h, pick_b = wf[0:64, 0:D], wf[0:64, 11816:11824], wf[0:64, 11824:11832]
        sp_ = view(wf, 10240, PAGES, NB * AH)
        sm = wf[0:NB * AH, 10752:11265]
        prod, dg, osum = wf[:, 11608:11672], wf[0:64, 11672:11736], view(wf, 11736, NB, AH)
        smc = wf[0:64, 11880:11884]
        kiT = view(wf, 4096, 2, SEQ)
        rel, scs, qiS = wf[0:32, 5120:5633], wf[0:NB, 5640:6153], wf[0:NB, 6200:6456]
        qiT, qm = view(wf, 6456, IH, NB), wf[:, 6488:6744].rearrange("p (c h b) -> p c h b", c=NB, h=IH)
        wd, lw, wcol = view(wf, 6744, IH, NB), wf[0:32, 6776:6784], wf[0:32, 6784:6785]
        prodi, fold, expand = view(wf, 6790, IH, NB), wf[0:32, 6830:6838], wf[0:NB, 6840:6904]
        xin, xin_s = view(wf, 0, QT, D), wf[:, 4096:5120]
        yout, yout_s = view(wf, 4160, QT, D), wf[:, 0:1024]

        acc = [ps[:, 0:2, 0:HALF], ps[:, 2:4, 0:HALF]]

        def halves(ap):
            return ap.rearrange("p (h t) -> p h t", h=2)

        def weights(stage, i, k):
            layer = int("".join(ch for ch in stage if ch.isdigit()))
            kind = kind_of(stage)
            if kind == "ret":
                if k < 12:
                    w = A["ret_w_in"][layer // 3].rearrange("(c p) n -> p c n", p=P)
                    part, c = [(0, k), (1, k - 2), (2, k - 4), (3, k - 8)][(k >= 2) + (k >= 4) + (k >= 8)]
                    wide = (RK, RK, RV, RV)[part]
                    return w[:, :, bass.ds(i * wide + ((0, D, 2 * D, 4 * D)[part] + c * P), P)]
                w = A["ret_w_out"][layer // 3].rearrange("(h c p) n -> h p c n", p=P, c=VC)
                if isinstance(i, int):
                    return w[i, :, :, (k - 12) * P:(k - 11) * P]
                return w[bass.ds(i, 1), :, :, (k - 12) * P:(k - 11) * P].rearrange("h p c n -> p (h c) n")
            if kind in ("up_a", "up_b"):
                w = A["ffn_w_in"][layer].rearrange("(c p) n -> p c n", p=P)
                col = (k % 2) * F + (FA if kind == "up_b" else 0) * P + (k // 2) * P
                return w[:, :, bass.ds(i * (2 * P) + col, P)]
            if kind in ("down_a", "down_b"):
                w = A["ffn_w_out"][layer].rearrange("(c p) n -> p c n", p=P)
                cs = slice(0, FA) if kind == "down_a" else slice(FA, FA + FB)
                return w[:, cs, k * P:(k + 1) * P]
            if kind == "pool":
                return A["pool_w_grp"][0, k].rearrange("(c p) n -> p c n", p=P)
            if kind == "proj":
                return A["dsa_w_out"][0].rearrange("(c p) n -> p c n", p=P)[:, :, k * P:(k + 1) * P]
            w = A["dsa_w_in"][0].rearrange("(c p) n -> p c n", p=P)
            if kind == "q":
                return w[:, :, k * P:(k + 1) * P]
            if kind == "kv":
                return w[:, :, bass.ds(i * (2 * P) + ((1 + k % 2) * D + (k // 2) * P), P)]
            if k < 2:
                return w[:, :, 3 * D + k * P:3 * D + (k + 1) * P]
            if k == 2:
                one = w[:, :, 3 * D + IH * ID:3 * D + IH * ID + ID]
                return one
            return w[:, :, 3 * D + IH * ID + ID + IH - P:3 * D + IH * ID + ID + IH]

        def columns(stage, i, k):
            kind = kind_of(stage)
            kc = {"ret": DC if k < 12 else VC, "up_a": DC, "up_b": DC, "down_a": FA, "down_b": FB,
                  "pool": 4, "idx": DC, "q": DC, "kv": DC, "proj": DC}[kind]
            return kc * P

        def slot_of(stage, k):
            return (marks.unit0[stage] + k) % 4

        def unit_mark(name, stage, i, k):
            return S[name], marks.unit(stage, i, k) + 1

        def load(sp, stage, i, k):
            src = weights(stage, i, k)
            n = slot_of(stage, k)
            dst = w_raw[:, n, 0:src.shape[1] * src.shape[2]].rearrange("p (c n) -> p c n", c=src.shape[1])
            sp.dma_start(dst, src).then_inc(S[f"w_in{n}"], 16)

        def landed(stage, k, n, m):
            if (kind_of(stage), k) == ("idx", 2):
                return w_raw[:, n, 0:DC * ID].rearrange("p (c n) -> p c n", c=DC).unsqueeze(2).broadcast_to([P, DC, 2, ID])
            return w_raw[:, n, 0:m]

        def whole(stage, k, ap):
            return ap.rearrange("p (c two n) -> p c two n", c=DC, two=2) if (kind_of(stage), k) == ("idx", 2) else ap

        def split_hi(act, stage, i, k):
            n, m = slot_of(stage, k), columns(stage, i, k)
            turn = (i * (marks.where[stage][1] // 4) + ((marks.unit0[stage] + k) // 4 + 1)) * 16
            act.wait_ge(S[f"w_in{n}"], turn)
            C.activation(whole(stage, k, w_h[:, n % 2, 0:m]), landed(stage, k, n, m), ACT.Copy).then_inc(S["w_hi"], 1)

        def split_lo(dve, stage, i, k):
            n, m = slot_of(stage, k), columns(stage, i, k)
            dve.wait_ge(*unit_mark("w_hi", stage, i, k))
            V.tensor_tensor(whole(stage, k, w_l[:, n % 2, 0:m]), landed(stage, k, n, m),
                            whole(stage, k, w_h[:, n % 2, 0:m].bitcast(F32)),
                            ALU.subtract).then_inc(S["w_lo"], 1)

        def split_next(which, eng, stage, i, k):
            then = marks.next_unit(stage, i, k + 2)
            if then:
                if which is split_hi:
                    eng.wait_ge(*unit_mark("mm", stage, i, k))
                which(eng, *then)

        def multiply(pe, stage, i, k, rhs_h, rhs_l, cs, part=None):
            n = slot_of(stage, k)
            part = part or range(cs)
            if part[0] == 0:
                pe.wait_ge(*unit_mark("w_lo", stage, i, k))
            wh = w_h[:, n % 2, :].rearrange("p (c n) -> p c n", n=P)
            wl = w_l[:, n % 2, :].rearrange("p (c n) -> p c n", n=P)
            for c in part:
                for lhs, rhs, term in ((wh, rhs_h, 0), (wh, rhs_l, 1), (wl, rhs_h, 2)):
                    for b, cols in enumerate(prompt_halves()):
                        mm = M.matmul(ps[:, 2 * (n % 2) + b, 0:HALF], lhs[:, c, :], rhs[:, c, cols],
                                      start=(c == 0 and term == 0), stop=(c == cs - 1 and term == 2))
            if part[-1] == cs - 1:
                mm.then_inc(S["mm"], 1)

        def multiply_first(pe, stage, rhs_h, rhs_l):
            at = marks.here(stage)
            pe.wait_ge(*unit_mark("w_lo", stage, 0, 1))
            for c in range(DC):
                pe.wait_ge(*at("x_lo", c + 1 - DC))
                for k in range(2):
                    n = slot_of(stage, k) % 2
                    wh = w_h[:, n, c * P:(c + 1) * P]
                    wl = w_l[:, n, c * P:(c + 1) * P]
                    for lhs, rhs, term in ((wh, rhs_h, 0), (wh, rhs_l, 1), (wl, rhs_h, 2)):
                        for b, cols in enumerate(prompt_halves()):
                            mm = M.matmul(ps[:, 2 * n + b, 0:HALF], lhs, rhs[:, c, cols],
                                          start=(c == 0 and term == 0), stop=(c == DC - 1 and term == 2))
                    if c == DC - 1:
                        mm.then_inc(S["mm"], 1)

        def three(out, lhs_h, lhs_l, rhs_h, rhs_l, start=True, stop=True):
            M.matmul(out, lhs_h, rhs_h, start=start, stop=False)
            M.matmul(out, lhs_h, rhs_l, start=False, stop=False)
            return M.matmul(out, lhs_l, rhs_h, start=False, stop=stop)

        def apart(eng):
            eng.wait_ge(S["tiny_c"], 2)

        def carry(eng):
            eng.sem_inc(S["carried"], 1)

        def page_of(eng, b, j):
            return eng.value_load(pages[0:1, bass.ds(b * PAGES + j, 1)], min_val=0, max_val=NPHYS - 1)

        def index_keys(eng, b):
            for j in range(PAGES):
                src = A["cache_kidx"][0][bass.ds(page_of(eng, b, j), 1)].rearrange("g s d -> s g d")
                eng.dma_start(kix[:, bass.ds(b * PAGES + j, 1), :], src).then_inc(S["kx_in"], 16)

        block = ctx.enter_context(nc.Block())

        @block.sync
        def _(sp):
            sp.dma_start(xin, A["x_prompt"][0].rearrange("(t p) d -> p t d", p=P)).then_inc(S["x_in"], 16)
            sp.dma_start(ident[:], A["ident"]).then_inc(S["x_in"], 16)
            sp.dma_start(xin_s[0:NB, :], A["x_sample"].rearrange("b o d -> (b o) d")).then_inc(S["x_in"], 16)
            stage0 = next(s for s, _, u in STAGES if u)
            for k in range(4):
                load(sp, stage0, 0, k)
            sp.dma_start(pages[:], A["page_table"].rearrange("b (o j) -> o (b j)", o=1)).then_inc(S["pages_in"], 16)
            sp.dma_start(rtab[:], A["ret_tab"].rearrange("a p t -> p a t")).then_inc(S["const"], 16)
            with nc.allow_non_contiguous_dma("columns of gains"):
                sp.dma_start(lncol[:, 0], A["ln_g"].rearrange("l s (c p) -> p (l s c)", p=P)).then_inc(S["const"], 16)
                sp.dma_start(lncol[:, 1], A["ln_b"].rearrange("l s (c p) -> p (l s c)", p=P)).then_inc(S["const"], 16)
            def page_loads(stage):
                at = marks.here(stage)
                for name in ("o_lo", "kv_out"):
                    sp.wait_ge(*at(name, 0))
                sp.dma_start(fold, A["fold"]).then_inc(S["pt_in"], 16)
                sp.dma_start(expand, A["expand"]).then_inc(S["pt_in"], 16)
                sp.dma_start(wf[0:64, 11816:11832], A["picks"]).then_inc(S["pt_in"], 16)
                sp.wait_ge(S["pages_in"], 16)

                def page(b, j):
                    return page_of(sp, b, j)

                with sp.Fori(0, NB // 2) as b:
                    index_keys(sp, b)
                with sp.Fori(0, NB // 2) as i:
                    for q in range(2):
                        for name in ("kr_v", "kr_a"):
                            sp.wait_ge(S[name], i * 4 + (marks.first[stage][name] + (q - 1) * 2))
                        if q:
                            sp.wait_ge(*at("b64", 2))
                        for j in range(PAGES):
                            src = A["cache_k"][0][bass.ds(page(i * 2 + q, j), 1)].rearrange("g s h d -> s g (h d)")
                            sp.dma_start(kvp[:, q, j:j + 1, :], src).then_inc(S[f"kp_in{q}"], 16)
                with sp.Fori(0, NB // 2) as i:
                    for q in range(2):
                        for name in ("kr_v", "kr_a"):
                            sp.wait_ge(*at(name, 14 + 2 * q))
                        sp.wait_ge(S["ov"], i * 2 + at("ov", q - 1)[1])
                        for j in range(PAGES):
                            src = A["cache_v"][0][bass.ds(page(i * 2 + q, j), 1)].rearrange("g s h d -> s g (h d)")
                            sp.dma_start(kvp[:, q, j:j + 1, :], src).then_inc(S[f"kp_in{q}"], 16)

            for stage, n, units in STAGES:
                if kind_of(stage) == "past":
                    page_loads(stage)
                for i in passes(sp, n) if units else ():
                    for k in range(units):
                        then = marks.next_unit(stage, i, k + 4)
                        if then:
                            sp.wait_ge(*unit_mark("w_lo", stage, i, k))
                            load(sp, *then)
            at = marks.here("end")
            sp.wait_ge(*at("y_cp", 16))
            sp.dma_start(O[0][0].rearrange("(t p) d -> p t d", p=P), yout).then_inc(S["y_out"], 16)
            sp.dma_start(O[1].rearrange("b o d -> (b o) d"), yout_s[0:NB, :]).then_inc(S["y_out"], 16)
            sp.wait_ge(S["y_out"], 32)
            for name in ("st_out0", "st_out1", "st_out2", "st_out3", "sf_out", "pl_out", "kv_out"):
                if marks.total[name]:
                    sp.wait_ge(S[name], marks.total[name])

        @block.gpsimd
        def _(pool):
            G.memset(qz, 0.0)
            G.memset(avg[:], 1.0 / D).then_inc(S["tiny_c"], 1)
            G.memset(mhalf, -0.5).then_inc(S["tiny_c"], 1)

            def ret(stage):
                j = int(stage[3:]) // 3
                s_in = A["state_ret"][j].rearrange("b h (d p) e -> h b p d e", p=P)
                s_out = O[3][j].rearrange("b h (d p) e -> h b p d e", p=P)

                def head(ap, i, b=None):
                    if isinstance(i, int):
                        return ap[i] if b is None else ap[i, b]
                    ap = ap[bass.ds(i, 1)]
                    return ap if b is None else ap[:, b]

                def to3(ap):
                    return ap if len(ap.shape) == 3 else ap.rearrange("h p d e -> p (h d) e")

                def to2(ap):
                    return ap if len(ap.shape) == 2 else ap.rearrange("h p n -> p (h n)")

                def head_constants(i):
                    carry(pool)
                    pool.dma_start(mask, to2(head(A["decay"], i))).then_inc(S["head_in"], 16)
                    pool.dma_start(headc[:, 0:8], to2(head(A["head_col"], i))).then_inc(S["head_in"], 16)
                    gains = A["ret_norm_g"][j].rearrange("(h c p) -> h p c", p=P, c=VC)
                    with nc.allow_non_contiguous_dma("columns of gains"):
                        pool.dma_start(headc[:, 8:12], to2(head(gains, i))).then_inc(S["head_in"], 16)

                def state_in(i, b):
                    carry(pool)
                    pool.dma_start(st[:, b % 4], to3(head(s_in, i, b))).then_inc(S[f"st_in{b % 4}"], 16)

                def rstd(at, t):
                    n = P if t < QT else NB
                    pool.wait_ge(*at("o_ag", t + 1))
                    carry(pool)
                    G.tensor_scalar(ve[0:n, t:t + 1], mv[0:n, t, 1:2], EPS, None, ALU.add).then_inc(S["rs_e"], 1)
                    pool.wait_ge(*at("rs_e", t + 1))
                    G.tensor_tensor(rs[0:n, t:t + 1], ve[0:n, t:t + 1], mhalf[0:n, :], ALU.pow).then_inc(S["rs_p"], 1)

                def state_out(at, i, b):
                    pool.wait_ge(*at("s_new", 2 * b + 2))
                    carry(pool)
                    pool.dma_start(to3(head(s_out, i, b)), st[:, b % 4]).then_inc(S[f"st_out{b % 4}"], 16)

                head_constants(0)
                for b in range(4):
                    state_in(0, b)
                for i in passes(pool, RH):
                    at = marks.here(stage, i)

                    def refill(b):
                        pool.wait_ge(*at(f"st_out{b % 4}", 16 * (1 + b // 4)))
                        pool.wait_ge(*at("so_mm", b + 1))
                        if b < 4:
                            state_in(i, b + 4)
                        elif not isinstance(i, int):
                            state_in(i + 1, b - 4)

                    rstd(at, 0)
                    rstd(at, 1)
                    state_out(at, i, 0)
                    state_out(at, i, 1)
                    rstd(at, 2)
                    rstd(at, 3)
                    refill(0)
                    refill(1)
                    state_out(at, i, 2)
                    state_out(at, i, 3)
                    refill(2)
                    refill(3)
                    for b in range(4, 8):
                        state_out(at, i, b)
                    rstd(at, 4)
                    for b in range(4, 8):
                        refill(b)
                    with_head = head(O[2][j, 0].rearrange("h (d p) e -> h p d e", p=P), i)
                    pool.wait_ge(*at("sf_cp", 2))
                    carry(pool)
                    pool.dma_start(to3(with_head), sf).then_inc(S["sf_out"], 32)
                    pool.wait_ge(*at("sf_out", 32))
                    if not isinstance(i, int):
                        pool.wait_ge(*at("gate_lo", 5))
                        head_constants(i + 1)

            def load_pool(stage):
                at = marks.here(stage)
                pool.wait_ge(*at("gate_lo", 0))
                pool.wait_ge(*at("so_mm", 0))
                for r in range(4):
                    pool.wait_ge(*at(f"st_out{r}", 0))
                pool.dma_start(hist[0:NB * HIST, :], A["state_pool"][0].rearrange("b t d -> (b t) d")
                               ).then_inc(S["pl_in"], 16)
                pool.dma_start(inv, A["inv_count"]).then_inc(S["pl_in"], 16)
                with nc.allow_non_contiguous_dma("columns of gains"):
                    pool.dma_start(headc[:, 0:DC], A["pool_scale"][0].rearrange("(c p) -> p c", p=P)
                                   ).then_inc(S["pl_in"], 16)

            def pool_out(stage):
                at = marks.here(stage)
                pool.wait_ge(*at("tail_cp", 2))
                pool.dma_start(O[4][0, 0], tail[0:HIST, :]).then_inc(S["pl_out"], 16)
                pool.dma_start(O[5][0, :, HIST - 1], tail[HIST:HIST + NB, :]).then_inc(S["pl_out"], 16)
                pool.dma_start(O[5][0, :, 0:HIST - 1], A["state_pool"][0][:, 1:HIST]).then_inc(S["pl_out"], 16)

            def load_tables(stage):
                at = marks.here(stage)
                for name in ("pl_out", "win", "d_lo", "y_sc"):
                    pool.wait_ge(*at(name, 0))
                for dst, src in ((dtab, A["dsa_tab"].rearrange("a p t -> p a t")), (itab, A["idx_tab"].rearrange("a p t -> p a t")),
                                 (rotm, A["dsa_rot"]), (roti, A["idx_rot"]), (causal, A["causal"])):
                    pool.dma_start(dst, src).then_inc(S["tab_in"], 16)

            def kidx_out(stage):
                at = marks.here(stage)
                pool.wait_ge(*at("ki_cp", 4))
                pool.dma_start(O[8][0, 0].rearrange("(t p) d -> p t d", p=P), kix_n).then_inc(S["kv_out"], 16)
                pool.dma_start(O[11][0, :, 0], kix_s).then_inc(S["kv_out"], 16)

            def kv_out(stage, n):
                for i in passes(pool, n):
                    at = marks.here(stage, i)
                    for q in range(2):
                        for w, (name, src, few) in enumerate((("kn_cp", kn, 6), ("vn_cp", vn, 7))):
                            pool.wait_ge(*at(name, 2 * q + 2))
                            cols = bass.ds(i * (2 * AD) + q * AD, AD)
                            full = O[few][0, 0].rearrange("(t p) h d -> p t (h d)", p=P)[:, :, cols]
                            carry(pool)
                            pool.dma_start(full, src).then_inc(S["kv_out"], 16)
                            new = O[few + 3][0, :, 0].rearrange("b h d -> b (h d)")[:, cols]
                            pool.dma_start(new, kvs[0:NB, w]).then_inc(S["kv_out"], 16)

            def centre(stage):
                at = marks.here(stage)
                pool.wait_ge(*at("sum_q", 0))
                pool.wait_ge(*at("ln_m", 1))
                for c in range(DC):
                    G.tensor_tensor(ln_e[:, c], x[:, c, :], ln_m, ALU.subtract).then_inc(S["ln_d"], 1)

            there = [s for s, _, _ in STAGES]
            for stage, n, units in STAGES:
                if kind_of(stage) == "norm":
                    centre(stage)
                    if stage == "norm0a" and "pool1" in there:
                        load_pool("pool1")
                    elif stage == "norm1a" and "idx2" in there:
                        load_tables("idx2")
                elif kind_of(stage) == "pool":
                    pool_out(stage)
                elif kind_of(stage) == "idx":
                    kidx_out(stage)
                elif kind_of(stage) == "kv":
                    kv_out(stage, n)
                elif kind_of(stage) == "ret":
                    last = "start" if stage == "ret0" else f"norm{int(stage[3:]) - 1}b"
                    pool.wait_ge(*marks.here(last)("x_lo", DC))
                    ret(stage)

        @block.scalar
        def _(act):
            def x_hi(at, c, ready):
                act.wait_ge(*at(ready, (c + 1) * (2 if ready == "x_t" else 1)))
                C.activation(x_h[:, c, :], x[:, c, :], ACT.Copy).then_inc(S["x_hi"], 1)

            def start(stage):
                at = marks.here(stage)
                act.wait_ge(*at("x_in", 48))
                C.activation(ident_r[:], ident[:], ACT.Copy).then_inc(S["idr"], 1)
                for c in range(DC):
                    x_hi(at, c, "x_t")
                for k in range(2):
                    split_hi(act, *marks.next_unit(next(s for s, _, u in STAGES if u), 0, k))

            def ret(stage):
                at0 = marks.here(stage)
                act.wait_ge(*at0("x_lo", 0))
                act.wait_ge(*at0("x_hi", 0))
                C.activation(x[:], x[:], ACT.Copy, scale=ALPHA).then_inc(S["xs"], 1)
                for i in passes(act, RH):
                    at = marks.here(stage, i)

                    def step(k, evacuate=None):
                        act.wait_ge(*unit_mark("mm", stage, i, k))
                        if evacuate:
                            evacuate()
                        split_next(split_hi, act, stage, i, k)

                    def raw_qk(n):
                        C.activation(halves(raw[:, n]), acc[n % 2], ACT.Copy,
                                     scale=1.0 if n < 2 else RK ** -0.5).then_inc(S["raw_qk"], 1)

                    def raw_v(n):
                        act.wait_ge(*at("rope", 8 if n >= 2 else 4))
                        C.activation(halves(raw[:, n]), acc[n % 2], ACT.Copy).then_inc(S["raw_v"], 1)

                    def silu_g(n):
                        C.activation(halves(sg[:, n]), acc[n % 2], ACT.Silu).then_inc(S["sil_g"], 1)

                    def qk_hi(n):
                        act.wait_ge(*at("rope", 4 * n + 4))
                        C.activation(qk_h[:, 2 * n:2 * n + 2], (q_f, k_f)[n], ACT.Copy).then_inc(S["qk_hi"], 1)

                    def kn_hi(t):
                        act.wait_ge(*at("kt", t // 2 + 1))
                        C.activation(kn_h[:, t], ps[:, 4 + t // 2, (t % 2) * RK:(t % 2 + 1) * RK], ACT.Copy,
                                     scale=headc[:, t:t + 1]).then_inc(S["kn_hi"], 1)

                    def v_hi(n):
                        act.wait_ge(*at("vt", n + 1))
                        if n < VC:
                            C.activation(v_h[:, 0:QT, n * P:(n + 1) * P], view(ps[:, VT_BANK[n]], 0, QT, P),
                                         ACT.Copy).then_inc(S["v_hi"], 1)
                        else:
                            C.activation(v_h[0:NB, QT, :], ps[0:NB, VT_BANK[n], :], ACT.Copy).then_inc(S["v_hi"], 1)

                    def att_hi(t):
                        act.wait_ge(*at("att_m", t + 1))
                        n = SEQ - t * P
                        C.activation(att_h[:, ATT_AT[t]:ATT_AT[t] + n], am[:, t % 2, 0:n], ACT.Copy
                                     ).then_inc(S["att_hi"], 1)

                    def scale_state(b):
                        act.wait_ge(*at(f"st_in{b % 4}", 16 * (b // 4 + 1)))
                        C.activation(st[:, b % 4], st[:, b % 4], ACT.Copy, scale=headc[:, 4:5]).then_inc(S["st_sc"], 1)

                    def gate_hi(t):
                        act.wait_ge(*at("gate_m", t + 1))
                        cols = slice(t * P, (t + 1) * P) if t < QT else slice(SEQ, T)
                        C.activation(gate_h[:, :, cols], sg[:, :, cols], ACT.Copy).then_inc(S["gate_hi"], 1)

                    def sf_copy(d):
                        act.wait_ge(*at("sf_mm", d + 1))
                        C.activation(sf[:, d], ps[:, SF_BANK[d]], ACT.Copy).then_inc(S["sf_cp"], 1)

                    step(0, lambda: raw_qk(0))
                    step(1, lambda: raw_qk(1))
                    qk_hi(0)
                    step(2, lambda: raw_qk(2))
                    step(3, lambda: raw_qk(3))
                    qk_hi(1)
                    step(4, lambda: raw_v(0))
                    act.wait_ge(*at("head_in", 48))
                    step(5, lambda: raw_v(1))
                    for t in range(QT):
                        kn_hi(t)
                    v_hi(0)
                    step(6, lambda: raw_v(2))
                    v_hi(1)
                    att_hi(0)
                    att_hi(1)
                    scale_state(0)
                    step(7, lambda: raw_v(3))
                    v_hi(2)
                    att_hi(2)
                    att_hi(3)
                    scale_state(1)
                    step(8, lambda: silu_g(0))
                    v_hi(3)
                    v_hi(4)
                    scale_state(2)
                    step(9, lambda: silu_g(1))
                    scale_state(3)
                    step(10, lambda: silu_g(2))
                    step(11, lambda: silu_g(3))
                    gate_hi(0)
                    gate_hi(1)
                    gate_hi(2)
                    gate_hi(3)
                    for b in range(4, 8):
                        scale_state(b)
                    sf_copy(0)
                    sf_copy(1)
                    gate_hi(4)
                    for k in range(12, 20):
                        step(k)
                        if k > 12 and isinstance(i, int):
                            square(marks.here(sums(stage)), marks.here(stage, i), k - 13)
                    if isinstance(i, int):
                        square(marks.here(sums(stage)), marks.here(stage, i), 7)

            def square(at, at_z, m):
                act.wait_ge(*at_z("z_add", m + 1))
                if m >= 2:
                    act.wait_ge(*at("sum_q", m - 1))
                C.activation(sq[:, m % 2], x[:, m, :], ACT.Square).then_inc(S["sq"], 1)

            def pooling(stage):
                at = marks.here(stage)
                act.wait_ge(*at("pl_in", 48))
                for b in range(2):
                    act.wait_ge(*at("pl_tail", b + 1))
                    C.activation(tail[0:HIST + NB, b * SEQ:(b + 1) * SEQ], ps[0:HIST + NB, 4 + b, :], ACT.Copy
                                 ).then_inc(S["tail_cp"], 1)
                def d_hi(g):
                    act.wait_ge(*at("win", POOL_OPS[g]))
                    C.activation(d_h[:, 2 * g:2 * g + 2], dd, ACT.Copy).then_inc(S["d_hi"], 1)

                d_hi(0)
                for g in range(4):
                    if g < 3:
                        d_hi(g + 1)
                    act.wait_ge(*unit_mark("mm", stage, 0, g))
                    for m in range(2):
                        if g:
                            act.wait_ge(*at("z_add", 2 * g - 1 + m))
                        C.activation(halves(ysc[:, m]), acc[m], ACT.Copy, scale=headc[:, 2 * g + m:2 * g + m + 1]
                                     ).then_inc(S["y_sc"], 1)
                    split_next(split_hi, act, stage, 0, g)
                    for m in range(2):
                        square(at, at, 2 * g + m)

            def d_copy(at, k, stage, i, unit, slot):
                act.wait_ge(*unit_mark("mm", stage, i, unit))
                C.activation(halves(d_raw[:, slot]), acc[unit % 2], ACT.Copy).then_inc(S["d_raw"], 1)

            def index(stage):
                at = marks.here(stage)
                for k in range(4):
                    if k >= 2:
                        act.wait_ge(*at("d_rope", 3 * (k - 2) + 3))
                    d_copy(at, k, stage, 0, k, k % 2)
                    split_next(split_hi, act, stage, 0, k)
                    if k < 3:
                        act.wait_ge(*at("d_rope", 3 * k + 3))
                        C.activation(qi_h[:, k, :] if k < 2 else ki_h, d_f[:, k % 2], ACT.Copy).then_inc(S["d_hi"], 1)
                act.wait_ge(*at("wi_tp", 1))
                C.activation(wi, view(ps[:, 6], 0, QT, P)[:, :, P - IH:P], ACT.Copy, scale=ISCALE).then_inc(S["ki_cp"], 1)
                C.activation(wi_s[0:NB, :], ps[0:NB, 7, P - IH:P], ACT.Copy, scale=ISCALE).then_inc(S["ki_cp"], 1)
                C.activation(kix_n, view(ps[:, 7], P, QT, ID), ACT.Copy).then_inc(S["ki_cp"], 1)
                C.activation(kix_s, ps[0:NB, 7, 384:448], ACT.Copy).then_inc(S["ki_cp"], 1)
                for n in range(12):
                    act.wait_ge(*at("s_idx", n + 1))
                    if n >= 2:
                        act.wait_ge(*at("sc", (n - 2) // 4 * 5 + (n - 2) % 4 + 1))
                    w = (n // 4 + 2) * P
                    C.activation(rl[:, n % 2, 0:w], ps[:, 4 + n % 4, 0:w], ACT.Relu).then_inc(S["rl"], 1)

            def queries(stage):
                at = marks.here(stage)
                for k in range(8):
                    act.wait_ge(*at("d_rope", 3 * (k - 2) + 3))
                    d_copy(at, k, stage, 0, k, k % 2)
                    split_next(split_hi, act, stage, 0, k)
                    act.wait_ge(*at("d_rope", 3 * k + 3))
                    C.activation(q_h[:, k, :], d_f[:, k % 2], ACT.Copy).then_inc(S["q_hi"], 1)

            def attend(stage, n):
                for i in passes(act, n):
                    at = marks.here(stage, i)
                    for q in range(2):
                        head = bass.ds(i * 2 + q, 1) if not isinstance(i, int) else slice(2 * i + q, 2 * i + q + 1)
                        act.wait_ge(*at("d_rope", 3 * q))
                        d_copy(at, 0, stage, i, 2 * q, 0)
                        split_next(split_hi, act, stage, i, 2 * q)
                        apart(act)
                        act.wait_ge(*at("pv", q))
                        C.activation(qa_h.rearrange("p (o t) -> p o t", o=1), q_h[:, head, :], ACT.Copy
                                     ).then_inc(S["qa_h"], 1)
                        act.wait_ge(*at("vv_tp", q))
                        d_copy(at, 1, stage, i, 2 * q + 1, 1)
                        split_next(split_hi, act, stage, i, 2 * q + 1)
                        act.wait_ge(*at("d_rope", 3 * q + 3))
                        C.activation(ka_h, d_f[:, 0], ACT.Copy).then_inc(S["k_hi"], 1)
                        act.wait_ge(*at("kv_out", 64 * q))
                        act.wait_ge(*at("kk_tp", q + 1))
                        C.activation(kn, view(ps[:, 6], 0, QT, P), ACT.Copy).then_inc(S["kn_cp"], 1)
                        C.activation(kvs[0:NB, 0], ps[0:NB, 4, 0:P], ACT.Copy).then_inc(S["kn_cp"], 1)
                        act.wait_ge(*at("vv_tp", q + 1))
                        C.activation(va_h, view(ps[:, 7], 0, QT, P), ACT.Copy).then_inc(S["vv_hi"], 1)
                        C.activation(vn, view(ps[:, 7], 0, QT, P), ACT.Copy).then_inc(S["vn_cp"], 1)
                        C.activation(kvs[0:NB, 1], ps[0:NB, 5, 0:P], ACT.Copy).then_inc(S["vn_cp"], 1)
                        for t in range(QT):
                            w, m = (t + 1) * P, 4 * q + t
                            act.wait_ge(*at("nmx", m + 1))
                            C.activation(pe_[:, t % 2, 0:w], pe_[:, t % 2, 0:w], ACT.Exp, bias=dnm[:, t:t + 1],
                                         accum_out=dsm[:, t:t + 1]).then_inc(S["p_exp"], 1)
                            if t:
                                p_hi(at, m - 1, t - 1)
                        p_hi(at, 4 * q + 3, 3)
                        apart(act)
                        act.wait_ge(*at("pv", q + 1))
                        C.activation(o_h[:, head, 0:SEQ], ps[:, 4:5, :], ACT.Copy).then_inc(S["o_hi"], 1)

            def past(stage):
                at = marks.here(stage)
                act.wait_ge(S["pages_in"], 16)
                act.wait_ge(*at("pt_in", 48))
                with act.Fori(NB // 2, NB) as b:
                    index_keys(act, b)
                for w in range(2):
                    act.wait_ge(*at("qi_t", w + 1))
                    if w == 0:
                        C.activation(qiS, ps[0:NB, 7, 0:2 * P], ACT.Copy).then_inc(S["qi_c"], 1)
                    else:
                        C.activation(qiT[0:ID], view(ps[:, 7], 256, IH, NB)[0:ID], ACT.Copy).then_inc(S["qi_c"], 1)
                act.wait_ge(*at("ki_w", 1))
                C.activation(wcol, ps[0:32, 7, 301:302], ACT.Copy, scale=float(D)).then_inc(S["wcol"], 1)
                for b in range(NB):
                    act.wait_ge(*at("kx_t", b + 1))
                    C.activation(kiT[0:ID, b % 2], ps[0:ID, 4 + b % 2, :], ACT.Copy).then_inc(S["kx_c"], 1)
                act.wait_ge(*at("kx_mm", 1))
                C.activation(rel[:, 0:PAST], ps[0:32, 6, :], ACT.Relu).then_inc(S["rel"], 1)
                C.activation(rel[:, PAST:PAST + 1], ps[0:32, 7, 300:301], ACT.Relu, scale=float(D)).then_inc(S["rel"], 1)
                act.wait_ge(*at("sc_mm", 1))
                C.activation(scs[:, 0:PAST], ps[0:NB, 5, :], ACT.Copy).then_inc(S["sc_cp"], 1)
                C.activation(scs[:, PAST:PAST + 1], ps[0:NB, 7, 302:303], ACT.Copy).then_inc(S["sc_cp"], 1)
                act.wait_ge(*at("b64_mm", 1))
                C.activation(sm[:, 0:PAST], ps[0:64, 4, :], ACT.Copy).then_inc(S["b64"], 1)
                C.activation(sm[:, PAST:PAST + 1], ps[0:64, 7, 303:304], ACT.Copy).then_inc(S["b64"], 1)
                for b in range(NB):
                    for j in (1, 3):
                        act.wait_ge(*at("kmm", 4 * b + j + 1))
                        for h in range(AH):
                            prods = kvp[:, b % 2, j, h * AD:(h + 1) * AD]
                            last = C.activation(prods, prods, ACT.Copy, accum_out=sp_[:, j, b * AH + h:b * AH + h + 1])
                        last.then_inc(S["kr_a"], 1)
                act.wait_ge(*at("smx", 2))
                C.activation(sm, sm, ACT.Exp, bias=smc[:, 1:2], scale=ASCALE, accum_out=smc[:, 2:3]).then_inc(S["sm_e"], 1)
                act.wait_ge(*at("osum", 2))
                C.activation(o_h[:, :, SEQ:T], osum.rearrange("p b h -> p h b"), ACT.Copy).then_inc(S["o_hi"], 1)

            def p_hi(at, m, t):
                w = (t + 1) * P
                act.wait_ge(*at("p_tp", m + 1))
                C.activation(p_h[:, t % 2, 0:w], ps[:, 4 + t, 0:w], ACT.Copy).then_inc(S["p_hi"], 1)

            def up(stage, n):
                for i in passes(act, n):
                    at = marks.here(stage, i)
                    for q in range(2):
                        act.wait_ge(*unit_mark("mm", stage, i, 2 * q))
                        C.activation(halves(sil[:, q]), acc[0], ACT.Silu).then_inc(S["sil"], 1)
                        split_next(split_hi, act, stage, i, 2 * q)
                        split_next(split_hi, act, stage, i, 2 * q + 1)
                        act.wait_ge(*at("h_raw", q + 1))
                        C.activation(h_h[:, bass.ds(i * 2 + q, 1), :] if not isinstance(i, int) else h_h[:, 2 * i + q:2 * i + q + 1, :],
                                     h_raw[:, q:q + 1], ACT.Copy).then_inc(S["h_hi"], 1)

            def down(stage, last):
                at = marks.here(stage)
                for k in range(8):
                    split_next(split_hi, act, stage, 0, k)
                    if last:
                        square(at, at, k)

            def norm(stage, which):
                at = marks.here(stage)
                act.wait_ge(*at("ln_v", 3))
                C.activation(ln_r, ln_r, ACT.Sqrt).then_inc(S["ln_sd"], 1)
                for c in range(DC):
                    act.wait_ge(*at("ln_e", c + 1))
                    col = which * DC + c
                    C.activation(x[:, c, :], ln_e[:, c], ACT.Identity, scale=lncol[:, 0, col:col + 1],
                                 bias=lncol[:, 1, col:col + 1]).then_inc(S["x_n"], 1)
                    x_hi(at, c, "x_n")

            for stage, n, units in STAGES:
                kind = kind_of(stage)
                layer = int("0" + "".join(ch for ch in stage if ch.isdigit()))
                if kind == "start":
                    start(stage)
                elif kind == "ret":
                    ret(stage)
                elif kind == "pool":
                    pooling(stage)
                elif kind == "idx":
                    index(stage)
                elif kind == "q":
                    queries(stage)
                elif kind == "kv":
                    attend(stage, n)
                elif kind == "past":
                    past(stage)
                elif kind in ("up_a", "up_b"):
                    up(stage, n)
                elif kind in ("down_a", "down_b", "proj"):
                    down(stage, kind != "down_a")
                elif kind == "norm":
                    norm(stage, 2 * layer + (stage[-1] == "b"))
                elif kind == "end":
                    at = marks.here(stage)
                    for name in ("st_out0", "st_out1", "st_out2", "st_out3", "sf_out", "pl_out"):
                        act.wait_ge(*at(name, 0))
                    for c in range(DC):
                        act.wait_ge(*at("y_tp", c + 1))
                        C.activation(yout[:, :, c * P:(c + 1) * P], view(ps[:, 4 + c % 2], 0, QT, P), ACT.Copy
                                     ).then_inc(S["y_cp"], 1)
                        act.wait_ge(*at("ys_tp", c + 1))
                        C.activation(yout_s[0:NB, c * P:(c + 1) * P], ps[0:NB, 6 + c % 2, 0:P], ACT.Copy
                                     ).then_inc(S["y_cp"], 1)

        @block.vector
        def _(dve):
            def x_lo(at, c):
                dve.wait_ge(*at("x_hi", c + 1))
                V.tensor_tensor(x_l[:, c, :], x[:, c, :], x_h[:, c, :].bitcast(F32), ALU.subtract
                                ).then_inc(S["x_lo"], 1)

            def start(stage):
                at = marks.here(stage)
                for name, head_start in HEAD_START.items():
                    dve.sem_inc(S[name], head_start)
                for c in range(DC):
                    dve.wait_ge(*at("xs_tp", c + 1))
                    V.tensor_copy(x[:, c, SEQ:T], ps[:, 6 + c % 2, 0:NB]).then_inc(S["x_t"], 1)
                    V.tensor_copy(x[:, c, 0:SEQ], ps[:, 4 + c % 2, :]).then_inc(S["x_t"], 1)
                    if c:
                        x_lo(at, c - 1)
                x_lo(at, DC - 1)
                for k in range(2):
                    split_lo(dve, *marks.next_unit(next(s for s, _, u in STAGES if u), 0, k))

            def add_up(at, m):
                if m == 0:
                    V.tensor_copy(sum_s, x[:, 0, :]).then_inc(S["sum_s"], 1)
                    dve.wait_ge(*at("sq", 1))
                    V.tensor_copy(sum_q, sq[:, 0]).then_inc(S["sum_q"], 1)
                    return
                dve.wait_ge(*at("sum_s", m))
                V.tensor_tensor(sum_s, sum_s, x[:, m, :], ALU.add).then_inc(S["sum_s"], 1)
                dve.wait_ge(*at("sq", m + 1))
                dve.wait_ge(*at("sum_q", m))
                V.tensor_tensor(sum_q, sum_q, sq[:, m % 2], ALU.add).then_inc(S["sum_q"], 1)

            def ret(stage):
                dve.wait_ge(*marks.here(stage)("const", 0))
                for i in passes(dve, RH):
                    at = marks.here(stage, i)

                    def rope(n):
                        dve.wait_ge(*at("raw_qk", 2 * n + 2))
                        f, two = (q_f, k_f)[n], raw[:, 2 * n:2 * n + 2]
                        cos = rtab[:, 0:1, :].to_broadcast([P, 2, T])
                        sin = rtab[:, 1:2, :].to_broadcast([P, 2, T])
                        V.tensor_tensor(f, two, cos, ALU.mult).then_inc(S["rope"], 1)
                        dve.wait_ge(*at("rope", 4 * n + 1))
                        V.tensor_tensor(two, two, sin, ALU.mult).then_inc(S["rope"], 1)
                        dve.wait_ge(*at("rope", 4 * n + 2))
                        V.tensor_tensor(f[:, 0], f[:, 0], two[:, 1], ALU.subtract).then_inc(S["rope"], 1)
                        V.tensor_tensor(f[:, 1], f[:, 1], two[:, 0], ALU.add).then_inc(S["rope"], 1)

                    def qk_lo(n):
                        dve.wait_ge(*at("qk_hi", n + 1))
                        V.tensor_tensor(qk_l[:, 2 * n:2 * n + 2], (q_f, k_f)[n],
                                        qk_h[:, 2 * n:2 * n + 2].bitcast(F32), ALU.subtract).then_inc(S["qk_lo"], 1)

                    def kn_lo(t):
                        dve.wait_ge(*at("kn_hi", t // 2 * 2 + 2))
                        V.scalar_tensor_tensor(kn_l[:, t], ps[:, 4 + t // 2, (t % 2) * RK:(t % 2 + 1) * RK],
                                               headc[:, t:t + 1], kn_h[:, t].bitcast(F32), ALU.mult, ALU.subtract
                                               ).then_inc(S["kn_lo"], 1)

                    def v_lo(n):
                        dve.wait_ge(*at("v_hi", n + 1))
                        if n < VC:
                            cols = slice(n * P, (n + 1) * P)
                            V.tensor_tensor(v_l[:, 0:QT, cols], view(ps[:, VT_BANK[n]], 0, QT, P),
                                            v_h[:, 0:QT, cols].bitcast(F32), ALU.subtract).then_inc(S["v_lo"], 1)
                        else:
                            V.tensor_tensor(v_l[0:NB, QT, :], ps[0:NB, VT_BANK[n], :],
                                            v_h[0:NB, QT, :].bitcast(F32), ALU.subtract).then_inc(S["v_lo"], 1)

                    def decay(t):
                        dve.wait_ge(*at("att", t + 1))
                        if t >= 2:
                            dve.wait_ge(*at("att_lo", t - 1))
                        n = SEQ - t * P
                        V.tensor_tensor(am[:, t % 2, 0:n], ps[:, AT_BANK[t], 0:n], mask[:, 0:n], ALU.mult
                                        ).then_inc(S["att_m"], 1)

                    def att_lo(t):
                        dve.wait_ge(*at("att_hi", t + 1))
                        n = SEQ - t * P
                        V.tensor_tensor(att_l[:, ATT_AT[t]:ATT_AT[t] + n], am[:, t % 2, 0:n],
                                        att_h[:, ATT_AT[t]:ATT_AT[t] + n].bitcast(F32), ALU.subtract
                                        ).then_inc(S["att_lo"], 1)

                    def gain(n):
                        dve.wait_ge(*at("sil_g", n + 1))
                        V.tensor_scalar(sg[:, n], sg[:, n], headc[:, 8 + n:9 + n], None, ALU.mult
                                        ).then_inc(S["sg_n"], 1)

                    def stats(t):
                        n = P if t < QT else NB
                        if t < QT:
                            dve.wait_ge(*at("o_mm", t + 1))
                        else:
                            dve.wait_ge(*at("so_mm", NB))
                        V.bn_stats(bn[0:n, t, :], ps[0:n, O_BANK[t], :]).then_inc(S["o_bn"], 1)
                        dve.wait_ge(*at("o_bn", t + 1))
                        carry(dve)
                        V.bn_aggr(mv[0:n, t, :], bn[0:n, t, :]).then_inc(S["o_ag"], 1)

                    def centre(t):
                        n = P if t < QT else NB
                        dve.wait_ge(*at("rs_p", t + 1))
                        dve.wait_ge(*at("o_ag", t + 1))
                        V.tensor_scalar(normed(t)[0:n], ps[0:n, O_BANK[t], :], mv[0:n, t, 0:1],
                                        rs[0:n, t:t + 1], ALU.subtract, ALU.mult).then_inc(S["o_n"], 1)

                    def gate(t):
                        dve.wait_ge(*at("ot", t + 1))
                        dve.wait_ge(*at("sg_n", 4))
                        cols, n = (slice(t * P, (t + 1) * P), P) if t < QT else (slice(SEQ, T), NB)
                        V.tensor_tensor(sg[:, :, cols], view(ps[:, OT_BANK[t]], 0, VC, n), sg[:, :, cols], ALU.mult
                                        ).then_inc(S["gate_m"], 1)

                    def gate_lo(t):
                        dve.wait_ge(*at("gate_hi", t + 1))
                        cols = slice(t * P, (t + 1) * P) if t < QT else slice(SEQ, T)
                        V.tensor_tensor(gate_l[:, :, cols], sg[:, :, cols], gate_h[:, :, cols].bitcast(F32),
                                        ALU.subtract).then_inc(S["gate_lo"], 1)

                    def new_state(b):
                        dve.wait_ge(*at("vb", b + 1))
                        dve.wait_ge(*at("st_sc", b + 1))
                        for d in range(KC):
                            V.scalar_tensor_tensor(st[:, b % 4, d], ps[:, 7, :], k_f[:, d, SEQ + b:SEQ + b + 1],
                                                   st[:, b % 4, d], ALU.mult, ALU.add).then_inc(S["s_new"], 1)

                    def step(k):
                        split_next(split_lo, dve, stage, i, k)

                    step(0)
                    step(1)
                    rope(0)
                    dve.wait_ge(*at("rope", 4))
                    for d in range(KC):
                        at_d = 64 + d * NB * NB
                        last = V.tensor_copy(tiny[:, at_d:at_d + NB * NB:NB + 1], q_f[:, d, SEQ:T])
                    last.then_inc(S["qs"], 1)
                    qk_lo(0)
                    step(2)
                    step(3)
                    rope(1)
                    qk_lo(1)
                    step(4)
                    dve.wait_ge(*at("head_in", 48))
                    step(5)
                    for t in range(QT):
                        kn_lo(t)
                    v_lo(0)
                    step(6)
                    v_lo(1)
                    decay(0)
                    decay(1)
                    att_lo(0)
                    att_lo(1)
                    step(7)
                    v_lo(2)
                    decay(2)
                    decay(3)
                    att_lo(2)
                    att_lo(3)
                    step(8)
                    v_lo(3)
                    v_lo(4)
                    gain(0)
                    step(9)
                    gain(1)
                    stats(0)
                    stats(1)
                    new_state(0)
                    centre(0)
                    centre(1)
                    step(10)
                    gain(2)
                    new_state(1)
                    stats(2)
                    stats(3)
                    centre(2)
                    centre(3)
                    new_state(2)
                    step(11)
                    gain(3)
                    new_state(3)
                    for t in range(QT):
                        gate(t)
                        if t:
                            gate_lo(t - 1)
                    gate_lo(3)
                    for b in range(4, 8):
                        new_state(b)
                    stats(4)
                    centre(4)
                    gate(4)
                    gate_lo(4)
                    last = isinstance(i, int)
                    for k in range(12, 20):
                        dve.wait_ge(*unit_mark("mm", stage, i, k))
                        V.tensor_tensor(halves(x[:, k - 12]), acc[k % 2], halves(x[:, k - 12]), ALU.add
                                        ).then_inc(S["z_add"], 1)
                        step(k)
                        if last:
                            dve.wait_ge(*at("z_add", k - 11))
                            add_up(marks.here(sums(stage)), k - 12)

            def pooling(stage):
                at = marks.here(stage)
                done = [0]

                def win_op(wait, issue):
                    if wait:
                        dve.wait_ge(*at("win", wait))
                    issue().then_inc(S["win"], 1)
                    done[0] += 1

                def residual(g):
                    if g == 0:
                        dve.wait_ge(*at("pl_tail", 2))
                    split_next(split_lo, dve, stage, 0, g)
                    for m in range(2):
                        dve.wait_ge(*at("y_sc", 2 * g + m + 1))
                        V.scalar_tensor_tensor(x[:, 2 * g + m], x[:, 2 * g + m], ALPHA, ysc[:, m], ALU.mult, ALU.add
                                               ).then_inc(S["z_add"], 1)
                        dve.wait_ge(*at("z_add", 2 * g + m + 1))
                        add_up(at, 2 * g + m)

                dve.wait_ge(*at("pl_in", 48))
                dve.wait_ge(*at("x_n", 0))
                for g, w in enumerate(WINDOWS):
                    xs = x[:, 2 * g:2 * g + 2, 0:SEQ]
                    xd = x[:, 2 * g:2 * g + 2, SEQ:T]
                    last = xs
                    for l in range(g + 1):
                        to, sh, n = win[l % 2], 2 ** l, done[0]
                        win_op(n, lambda: V.tensor_tensor(to[:, :, sh:SEQ], last[:, :, sh:SEQ], last[:, :, 0:SEQ - sh],
                                                          ALU.add))
                        win_op(0, lambda: V.tensor_copy(to[:, :, 0:sh], last[:, :, 0:sh]))
                        last = to
                    n = done[0]
                    if g:
                        dve.wait_ge(*at("d_lo", g))
                    table = inv[:, 16 * g:16 * g + 16].rearrange("p (o t) -> p o t", o=1).to_broadcast([P, 2, 16])
                    win_op(n, lambda: V.scalar_tensor_tensor(dd[:, :, 16:SEQ], last[:, :, 16:SEQ], 1.0 / w,
                                                             xs[:, :, 16:SEQ], ALU.mult, ALU.subtract))
                    win_op(0, lambda: V.tensor_tensor(dd[:, :, 0:16], last[:, :, 0:16], table, ALU.mult))
                    dve.wait_ge(*at("pl_hist", 2))
                    past = ps[:, 6 + g // 2, (g % 2) * 240:(g % 2) * 240 + 240].rearrange("p (c b t) -> p c b t", c=2, b=NB)
                    for c in range(2):
                        win_op(0, lambda: V.tensor_reduce(dd[:, c, SEQ:T], past[:, c, :, HIST - w + 1:HIST], AX.X, ALU.add))
                    n = done[0]
                    win_op(n, lambda: V.tensor_tensor(dd[:, :, 0:16], dd[:, :, 0:16], xs[:, :, 0:16], ALU.subtract))
                    win_op(0, lambda: V.tensor_tensor(dd[:, :, SEQ:T], dd[:, :, SEQ:T], xd, ALU.add))
                    n = done[0]
                    win_op(n, lambda: V.scalar_tensor_tensor(dd[:, :, SEQ:T], dd[:, :, SEQ:T], 1.0 / w, xd, ALU.mult,
                                                             ALU.subtract))
                    assert done[0] == POOL_OPS[g], done
                    dve.wait_ge(*at("d_hi", g + 1))
                    V.tensor_tensor(d_l[:, 2 * g:2 * g + 2], dd, d_h[:, 2 * g:2 * g + 2].bitcast(F32), ALU.subtract
                                    ).then_inc(S["d_lo"], 1)
                    if g:
                        residual(g - 1)
                residual(3)

            def d_rotate(at, k, tab, slot, to):
                dve.wait_ge(*at("rot", k + 1))
                dve.wait_ge(*at("d_rope", 3 * k))
                V.tensor_tensor(halves(d_t), ps[:, 4:6, 0:HALF], halves(tab[:, 1]), ALU.mult).then_inc(S["d_rope"], 1)
                V.tensor_tensor(d_f[:, to], d_raw[:, slot], tab[:, 0], ALU.mult).then_inc(S["d_rope"], 1)
                dve.wait_ge(*at("d_rope", 3 * k + 2))
                V.tensor_tensor(d_f[:, to], d_f[:, to], d_t, ALU.add).then_inc(S["d_rope"], 1)

            def index(stage):
                at = marks.here(stage)
                dve.wait_ge(*at("tab_in", 80))
                for k in range(4):
                    split_next(split_lo, dve, stage, 0, k)
                    if k < 3:
                        d_rotate(at, k, itab, k % 2, k % 2)
                        dve.wait_ge(*at("d_rope", 3 * k + 3))
                        keep = qi_d[:, k] if k < 2 else ki_d
                        V.tensor_copy(keep, d_f[:, k % 2, SEQ:T]).then_inc(S["sv_i"], 1)
                        dve.wait_ge(*at("d_hi", k + 1))
                        hi, lo = (qi_h[:, k, :], qi_l[:, k, :]) if k < 2 else (ki_h, ki_l)
                        V.tensor_tensor(lo, d_f[:, k % 2], hi.bitcast(F32), ALU.subtract).then_inc(S["d_lo"], 1)
                dve.wait_ge(*at("ki_cp", 4))
                for n in range(12):
                    t, h = n // 4 + 1, n % 4
                    w, to, ev = (t + 1) * P, SC_AT[t], (t - 1) * 5 + h
                    dve.wait_ge(*at("rl", n + 1))
                    if h == 0:
                        V.tensor_scalar(sc[:, to:to + w], rl[:, n % 2, 0:w], wi[:, t, 0:1], None, ALU.mult
                                        ).then_inc(S["sc"], 1)
                    else:
                        dve.wait_ge(*at("sc", ev))
                        V.scalar_tensor_tensor(sc[:, to:to + w], rl[:, n % 2, 0:w], wi[:, t, h:h + 1], sc[:, to:to + w],
                                               ALU.mult, ALU.add).then_inc(S["sc"], 1)
                    if h == 3:
                        dve.wait_ge(*at("sc", ev + 1))
                        V.tensor_tensor(sc[:, to + t * P:to + w], sc[:, to + t * P:to + w], causal, ALU.add
                                        ).then_inc(S["sc"], 1)

            def queries(stage):
                at = marks.here(stage)

                def pick(r):
                    t, ev = r // 16 + 1, 2 * r
                    s_t = sc[:, SC_AT[t]:SC_AT[t] + (t + 1) * P]
                    dve.wait_ge(*(at("pick", ev) if ev else at("sc", 0)))
                    V.max(mx8, s_t).then_inc(S["pick"], 1)
                    dve.wait_ge(*at("pick", ev + 1))
                    V.match_replace(s_t, mx8, s_t, GONE).then_inc(S["pick"], 1)

                for k in range(8):
                    split_next(split_lo, dve, stage, 0, k)
                    d_rotate(at, k, dtab, k % 2, k % 2)
                    dve.wait_ge(*at("d_rope", 3 * k + 3))
                    V.tensor_copy(qs_d[:, k], d_f[:, k % 2, SEQ:T]).then_inc(S["qs_cp"], 1)
                    dve.wait_ge(*at("q_hi", k + 1))
                    V.tensor_tensor(q_l[:, k], d_f[:, k % 2], q_h[:, k].bitcast(F32), ALU.subtract).then_inc(S["q_lo"], 1)
                    for r in range(6):
                        pick(6 * k + r)
                V.tensor_copy(bias[:, 0:P], causal).then_inc(S["bias"], 1)
                dve.wait_ge(*at("pick", 96))
                for t in range(1, QT):
                    w = (t + 1) * P
                    V.tensor_scalar(bias[:, BIAS_AT[t]:BIAS_AT[t] + w], sc[:, SC_AT[t]:SC_AT[t] + w], 0.5 * GONE, -BIG,
                                    ALU.is_gt, ALU.mult).then_inc(S["bias"], 1)
                dve.wait_ge(*at("bias", 4))

            def attend(stage, n):
                dve.wait_ge(*marks.here(stage)("kv_out", 0))
                for i in passes(dve, n):
                    at = marks.here(stage, i)
                    for q in range(2):
                        head = bass.ds(i * 2 + q, 1) if not isinstance(i, int) else slice(2 * i + q, 2 * i + q + 1)
                        split_next(split_lo, dve, stage, i, 2 * q)
                        dve.wait_ge(*at("qa_h", q + 1))
                        V.tensor_copy(qa_l.rearrange("p (o t) -> p o t", o=1), q_l[:, head, :].bitcast(F32)
                                      ).then_inc(S["qa_l"], 1)
                        d_rotate(at, q, dtab, 0, 0)
                        dve.wait_ge(*at("d_rope", 3 * q + 3))
                        V.tensor_copy(ks_d[:, head], d_f[:, 0:1, SEQ:T]).then_inc(S["ks_cp"], 1)
                        dve.wait_ge(*at("k_hi", q + 1))
                        V.tensor_tensor(ka_l, d_f[:, 0], ka_h.bitcast(F32), ALU.subtract).then_inc(S["k_lo"], 1)
                        split_next(split_lo, dve, stage, i, 2 * q + 1)
                        dve.wait_ge(*at("d_raw", 2 * q + 2))
                        V.tensor_copy(vs_d[:, head], d_raw[:, 1:2, SEQ:T]).then_inc(S["ks_cp"], 1)
                        dve.wait_ge(*at("vn_cp", 2 * q + 2))
                        V.tensor_tensor(va_l, view(ps[:, 7], 0, QT, P), va_h.bitcast(F32), ALU.subtract
                                        ).then_inc(S["vv_lo"], 1)
                        for t in range(QT):
                            w, m, to = (t + 1) * P, 4 * q + t, BIAS_AT[t]
                            dve.wait_ge(*at("s_mm", m + 1))
                            if t >= 2:
                                dve.wait_ge(*at("p_tp", m - 1))
                            carry(dve)
                            V.tensor_tensor_reduce(out=pe_[:, t % 2, 0:w], in0=ps[:, 4 + t, 0:w], in1=bias[:, to:to + w],
                                                   scale=ASCALE, scalar=-3.0e38, op0=ALU.add, op1=ALU.max,
                                                   accum_out=dmx[:, t:t + 1]).then_inc(S["s_sc"], 1)
                            dve.wait_ge(*at("s_sc", m + 1))
                            V.tensor_scalar(dnm[:, t:t + 1], dmx[:, t:t + 1], -1.0, None, ALU.mult).then_inc(S["nmx"], 1)
                            dve.wait_ge(*at("p_exp", m + 1))
                            V.reciprocal(drc[:, t:t + 1], dsm[:, t:t + 1]).then_inc(S["p_rc"], 1)
                            dve.wait_ge(*at("p_rc", m + 1))
                            V.tensor_scalar(pe_[:, t % 2, 0:w], pe_[:, t % 2, 0:w], drc[:, t:t + 1], None, ALU.mult
                                            ).then_inc(S["p_n"], 1)
                            if t:
                                p_lo(at, m - 1, t - 1)
                        p_lo(at, 4 * q + 3, 3)
                        dve.wait_ge(*at("o_hi", q + 1))
                        V.tensor_tensor(o_l[:, head, 0:SEQ], ps[:, 4:5, :], o_h[:, head, 0:SEQ].bitcast(F32), ALU.subtract
                                        ).then_inc(S["o_lo"], 1)

            def past(stage):
                at = marks.here(stage)
                dve.wait_ge(*at("pt_in", 48))
                V.memset(qm[0:ID], 0.0).then_inc(S["qm"], 1)
                for h in range(IH):
                    V.tensor_scalar(wd[0:NB, h], ident[0:NB, 0:NB], wi_s[0:NB, h:h + 1], None, ALU.mult).then_inc(S["qm"], 1)
                dve.wait_ge(*at("qm", 1))
                dve.wait_ge(*at("qi_c", 2))
                for b in range(NB):
                    V.tensor_copy(qm[0:ID, b, :, b:b + 1], qiT[0:ID, :, b:b + 1]).then_inc(S["qm"], 1)
                new = ki_d[0:ID].rearrange("p (o b) -> p o b", o=1).to_broadcast([ID, IH, NB])
                V.tensor_tensor(prodi[0:ID], qiT[0:ID], new, ALU.mult).then_inc(S["prodi"], 1)
                dve.wait_ge(*at("wcol", 1))
                V.tensor_scalar(lw, fold, wcol, None, ALU.mult).then_inc(S["lw"], 1)
                def products(n):
                    b, j = n // PAGES, n % PAGES
                    if j == 0:
                        dve.wait_ge(*at(f"kp_in{b % 2}", 64 * (b // 2 + 1)))
                        dve.wait_ge(*at("qc", b + 1))
                    keys = kvp[:, b % 2, j, :].rearrange("p (a n) -> p a n", a=2)
                    V.tensor_tensor(keys, keys, ps[:, 2 * (b % 2):2 * (b % 2) + 2, :], ALU.mult).then_inc(S["kmm"], 1)

                def page_step(n):
                    b, j = n // PAGES, n % PAGES
                    products(n)
                    if n and j % 2:
                        dve.wait_ge(*at("kmm", n))
                        V.tensor_reduce(sp_[:, j - 1, b * AH:(b + 1) * AH],
                                        kvp[:, b % 2, j - 1, :].rearrange("p (h d) -> p h d", h=AH), AX.X, ALU.add
                                        ).then_inc(S["kr_v"], 1)

                for n in range(PAGES):
                    page_step(n)
                dve.wait_ge(*at("sc_cp", 2))
                for r in range(TOPK // 8):
                    if r:
                        dve.wait_ge(*at("sp_pick", 2 * r))
                    V.max(mx8[0:NB], scs).then_inc(S["sp_pick"], 1)
                    dve.wait_ge(*at("sp_pick", 2 * r + 1))
                    V.match_replace(scs, mx8[0:NB], scs, GONE).then_inc(S["sp_pick"], 1)
                dve.wait_ge(*at("sp_pick", 32))
                V.tensor_scalar(scs, scs, 0.5 * GONE, -BIG, ALU.is_gt, ALU.mult).then_inc(S["sp_pick"], 1)
                V.tensor_tensor(prod.rearrange("p (b h) -> p b h", b=NB), qs_d.rearrange("p h b -> p b h"),
                                ks_d.rearrange("p h b -> p b h"), ALU.mult).then_inc(S["pr"], 1)
                dve.wait_ge(*at("b64", 2))
                V.memset(wf[:, 8192:10240], 0.0).then_inc(S["pz"], 1)

                for n in range(PAGES, NB * PAGES):
                    page_step(n)
                dve.wait_ge(*at("s64", 1))
                V.tensor_tensor(sm[:, 0:PAST], ps[0:64, 6, :], sm[:, 0:PAST], ALU.add).then_inc(S["sm"], 1)
                V.scalar_tensor_tensor(sm[:, PAST:PAST + 1], ps[0:64, 7, 0:1], float(D), sm[:, PAST:PAST + 1],
                                       ALU.mult, ALU.add).then_inc(S["sm"], 1)
                dve.wait_ge(*at("sm", 2))
                V.reduce_max(smc[:, 0:1], sm, AX.X).then_inc(S["smx"], 1)
                dve.wait_ge(*at("smx", 1))
                V.tensor_scalar(smc[:, 1:2], smc[:, 0:1], -ASCALE, None, ALU.mult).then_inc(S["smx"], 1)
                dve.wait_ge(*at("sm_e", 1))
                V.reciprocal(smc[:, 3:4], smc[:, 2:3]).then_inc(S["sm_n"], 1)
                dve.wait_ge(*at("sm_n", 1))
                V.tensor_scalar(sm, sm, smc[:, 3:4], None, ALU.mult).then_inc(S["sm_n"], 1)
                dve.wait_ge(*at("sm_n", 2))
                V.tensor_scalar(dg, ident[0:64, 0:64], sm[:, PAST:PAST + 1], None, ALU.mult).then_inc(S["dg"], 1)
                dve.wait_ge(*at("pt_t", 1))
                V.scalar_tensor_tensor(osum, view(ps[:, 7], 64, NB, AH), float(D), vs_d.rearrange("p h b -> p b h"),
                                       ALU.mult, ALU.mult).then_inc(S["osum"], 1)
                dve.wait_ge(*at("pz", 1))
                for b in range(NB):
                    V.tensor_copy(pz[:, :, b, b * AH:(b + 1) * AH], view(ps[:, 6], 0, PAGES, 64)[:, :, b * AH:(b + 1) * AH]
                                  ).then_inc(S["pc"], 1)
                dve.wait_ge(*at("ov", NB))
                V.tensor_tensor(om.rearrange("p (a h d) -> p a h d", a=2, h=AH // 2),
                                ps[0:64, 4:6, :].rearrange("p a (h d) -> p a h d", h=AH // 2),
                                pick_h.rearrange("p (a h) -> p a h", a=2).unsqueeze(3).broadcast_to([64, 2, AH // 2, AD]),
                                ALU.mult).then_inc(S["om"], 1)
                dve.wait_ge(*at("oh", 1))
                dve.wait_ge(*at("osum", 1))
                V.tensor_tensor(osum, ps[:, 6, 0:64].rearrange("p (h b) -> p b h", h=AH), osum, ALU.add
                                ).then_inc(S["osum"], 1)
                dve.wait_ge(*at("o_hi", 1))
                V.tensor_tensor(o_l[:, :, SEQ:T], osum.rearrange("p b h -> p h b"), o_h[:, :, SEQ:T].bitcast(F32),
                                ALU.subtract).then_inc(S["o_lo"], 1)

            def p_lo(at, m, t):
                w = (t + 1) * P
                dve.wait_ge(*at("p_hi", m + 1))
                V.tensor_tensor(p_l[:, t % 2, 0:w], ps[:, 4 + t, 0:w], p_h[:, t % 2, 0:w].bitcast(F32), ALU.subtract
                                ).then_inc(S["p_lo"], 1)

            def up(stage, n):
                for i in passes(dve, n):
                    at = marks.here(stage, i)
                    for q in range(2):
                        split_next(split_lo, dve, stage, i, 2 * q)
                        dve.wait_ge(*at("sil", q + 1))
                        dve.wait_ge(*unit_mark("mm", stage, i, 2 * q + 1))
                        dve.wait_ge(*at("h_lo", q - 1))
                        V.tensor_tensor(halves(h_raw[:, q]), acc[1], halves(sil[:, q]), ALU.mult).then_inc(S["h_raw"], 1)
                        split_next(split_lo, dve, stage, i, 2 * q + 1)
                        dve.wait_ge(*at("h_hi", q + 1))
                        at_m = bass.ds(i * 2 + q, 1) if not isinstance(i, int) else slice(2 * i + q, 2 * i + q + 1)
                        V.tensor_tensor(h_l[:, at_m, :], h_raw[:, q:q + 1], h_h[:, at_m, :].bitcast(F32),
                                        ALU.subtract).then_inc(S["h_lo"], 1)

            def down(stage, kind):
                at = marks.here(stage)
                for k in range(8):
                    dve.wait_ge(*unit_mark("mm", stage, 0, k))
                    if kind == "down_b":
                        V.tensor_tensor(halves(x[:, k]), acc[k % 2], halves(x[:, k]), ALU.add).then_inc(S["z_add"], 1)
                    else:
                        V.scalar_tensor_tensor(halves(x[:, k]), halves(x[:, k]), ALPHA, acc[k % 2], ALU.mult, ALU.add
                                               ).then_inc(S["z_add"], 1)
                    split_next(split_lo, dve, stage, 0, k)
                    if kind != "down_a":
                        dve.wait_ge(*at("z_add", k + 1))
                        add_up(at, k)

            def norm(stage):
                at = marks.here(stage)
                dve.wait_ge(*at("stat", 2))
                V.tensor_copy(halves(ln_m), ps[:, 4:6, 0:HALF]).then_inc(S["ln_m"], 1)
                dve.wait_ge(*at("ln_m", 1))
                V.tensor_tensor(ln_r, ln_m, ln_m, ALU.mult).then_inc(S["ln_v"], 1)
                dve.wait_ge(*at("stat", 4))
                dve.wait_ge(*at("ln_v", 1))
                V.scalar_tensor_tensor(halves(ln_r), halves(ln_r), -1.0, ps[:, 6:8, 0:HALF], ALU.mult, ALU.add
                                       ).then_inc(S["ln_v"], 1)
                dve.wait_ge(*at("ln_v", 2))
                V.tensor_scalar(ln_r, ln_r, 0.0, EPS, ALU.max, ALU.add).then_inc(S["ln_v"], 1)
                dve.wait_ge(*at("ln_sd", 1))
                V.reciprocal(ln_r, ln_r).then_inc(S["ln_rs"], 1)
                for c in range(DC):
                    dve.wait_ge(*at("ln_d", c + 1))
                    dve.wait_ge(*at("ln_rs", 1))
                    V.tensor_tensor(ln_e[:, c], ln_e[:, c], ln_r, ALU.mult).then_inc(S["ln_e"], 1)
                    if c:
                        x_lo(at, c - 1)
                x_lo(at, DC - 1)

            for stage, n, units in STAGES:
                kind = kind_of(stage)
                if kind == "start":
                    start(stage)
                elif kind == "ret":
                    ret(stage)
                elif kind == "pool":
                    pooling(stage)
                elif kind == "idx":
                    index(stage)
                elif kind == "q":
                    queries(stage)
                elif kind == "kv":
                    attend(stage, n)
                elif kind == "past":
                    past(stage)
                elif kind in ("up_a", "up_b"):
                    up(stage, n)
                elif kind in ("down_a", "down_b", "proj"):
                    down(stage, kind)
                elif kind == "norm":
                    norm(stage)

        @block.tensor
        def _(pe):
            def turn(out, src, n):
                return M.transpose(out, src, ident[0:n, 0:n])

            def start(stage):
                at = marks.here(stage)
                pe.wait_ge(*at("x_in", 48))
                for c in range(DC):
                    if c >= 2:
                        pe.wait_ge(*at("x_t", 2 * c - 2))
                    for t in range(QT):
                        mm = turn(ps[:, 4 + c % 2, t * P:(t + 1) * P], xin[:, t, c * P:(c + 1) * P], P)
                    mm.then_inc(S["x_tp"], 1)
                    turn(ps[:, 6 + c % 2, 0:NB], xin_s[0:NB, c * P:(c + 1) * P], NB).then_inc(S["xs_tp"], 1)

            def ret(stage):
                for i in passes(pe, RH, 1):
                    at = marks.here(stage, i)

                    def unit(k):
                        before = [("z_add", -1), ("z_add", 0)] + [("raw_qk", n + 1) for n in range(4)] + [
                            ("raw_v", n + 1) for n in range(4)] + [("sil_g", n + 1) for n in range(4)] + [
                            ("z_add", n + 1) for n in range(6)]
                        pe.wait_ge(*at(*before[k]))
                        if k < 12:
                            multiply(pe, stage, i, k, x_h, x_l, DC)
                        else:
                            multiply(pe, stage, i, k, gate_h, gate_l, VC)

                    def keys(n):
                        pe.wait_ge(*at("rope", 8))
                        for t in (2 * n, 2 * n + 1):
                            for d in range(KC):
                                mm = turn(ps[:, 4 + n, (t % 2) * RK + d * P:(t % 2) * RK + (d + 1) * P],
                                          k_f[:, d, t * P:(t + 1) * P], P)
                        mm.then_inc(S["kt"], 1)

                    def values(n, free):
                        pe.wait_ge(*at("raw_v", min(n + 1, VC)))
                        if free:
                            pe.wait_ge(*at(*free))
                        if n < VC:
                            for t in range(QT):
                                mm = turn(ps[:, VT_BANK[n], t * P:(t + 1) * P], raw[:, n, t * P:(t + 1) * P], P)
                        else:
                            for c in range(VC):
                                mm = turn(ps[0:NB, VT_BANK[n], c * P:(c + 1) * P], raw[:, c, SEQ:T], P)
                        mm.then_inc(S["vt"], 1)

                    def scores(t, free):
                        pe.wait_ge(*at("qk_lo", 2))
                        pe.wait_ge(*at(*free))
                        n, keys_at, later = SEQ - t * P, slice(t * P, (t + 1) * P), slice(t * P, SEQ)
                        for d in range(KC):
                            mm = three(ps[:, AT_BANK[t], 0:n], qk_h[:, 2 + d, keys_at], qk_l[:, 2 + d, keys_at],
                                       qk_h[:, d, later], qk_l[:, d, later], d == 0, d == KC - 1)
                        mm.then_inc(S["att"], 1)

                    def outputs(t, free):
                        pe.wait_ge(*at("v_lo", free[1] if free[0] == "v_lo" else 4))
                        pe.wait_ge(*at("att_lo", 4))
                        if free[0] != "v_lo":
                            pe.wait_ge(*at(*free))
                        for j in range(t + 1):
                            a = ATT_AT[j] + (t - j) * P
                            mm = three(ps[:, O_BANK[t], :], att_h[:, a:a + P], att_l[:, a:a + P], v_h[:, j], v_l[:, j],
                                       j == 0, j == t)
                        mm.then_inc(S["o_mm"], 1)

                    def turn_outputs(t, free):
                        pe.wait_ge(*at("o_n", max(t + 1, free[1]) if free[0] == "o_n" else t + 1))
                        if free[0] != "o_n":
                            pe.wait_ge(*at(*free))
                        carry(pe)
                        n = P if t < QT else NB
                        for c in range(VC):
                            mm = turn(ps[:, OT_BANK[t], c * n:(c + 1) * n], normed(t)[0:n, c * P:(c + 1) * P], n)
                        mm.then_inc(S["ot"], 1)

                    def final_state(d, free):
                        pe.wait_ge(*at(*free))
                        pe.wait_ge(*at("kn_lo", 4))
                        for t in range(QT):
                            mm = three(ps[:, SF_BANK[d], :], kn_h[:, t, d * P:(d + 1) * P], kn_l[:, t, d * P:(d + 1) * P],
                                       v_h[:, t], v_l[:, t], t == 0, t == QT - 1)
                        mm.then_inc(S["sf_mm"], 1)

                    def spread_v(b):
                        pe.wait_ge(*at("v_lo", 5))
                        if b:
                            pe.wait_ge(*at("s_new", 2 * b))
                        one = ident_r[0:NB, b:b + 1].to_broadcast([NB, P])
                        M.matmul(ps[:, 7, :], one, v_h[0:NB, QT, :], start=True, stop=False)
                        M.matmul(ps[:, 7, :], one, v_l[0:NB, QT, :], start=False, stop=True).then_inc(S["vb"], 1)

                    def read_state(b):
                        pe.wait_ge(*at("s_new", 2 * b + 2))
                        pe.wait_ge(*at("qs", 1))
                        for d in range(KC):
                            mm = M.matmul(ps[0:NB, 6, :], qz[:, d, b, :], st[:, b % 4, d, :], start=(b + d == 0),
                                          stop=(b == NB - 1 and d == KC - 1))
                        mm.then_inc(S["so_mm"], 1)

                    if isinstance(i, int) and i == 0:
                        pe.wait_ge(*at("z_add", 0))
                        multiply_first(pe, stage, x_h, x_l)
                    else:
                        unit(0)
                        unit(1)
                    for k in range(2, 6):
                        unit(k)
                    keys(0)
                    keys(1)
                    values(0, ())
                    unit(6)
                    values(1, ())
                    scores(0, ("kn_lo", 2))
                    scores(1, ("kn_lo", 4))
                    unit(7)
                    values(2, ("att_m", 1))
                    scores(2, ("v_lo", 1))
                    scores(3, ("v_lo", 2))
                    unit(8)
                    values(3, ("att_m", 2))
                    values(4, ("v_lo", 3))
                    unit(9)
                    outputs(0, ("v_lo", 4))
                    outputs(1, ("v_lo", 5))
                    spread_v(0)
                    unit(10)
                    spread_v(1)
                    outputs(2, ("o_n", 1))
                    outputs(3, ("o_n", 2))
                    read_state(0)
                    spread_v(2)
                    unit(11)
                    read_state(1)
                    spread_v(3)
                    turn_outputs(0, ("o_n", 3))
                    turn_outputs(1, ("o_n", 4))
                    read_state(2)
                    spread_v(4)
                    turn_outputs(2, ("gate_m", 1))
                    turn_outputs(3, ("gate_m", 2))
                    read_state(3)
                    spread_v(5)
                    final_state(0, ("gate_m", 3))
                    read_state(4)
                    spread_v(6)
                    read_state(5)
                    spread_v(7)
                    read_state(6)
                    read_state(7)
                    final_state(1, ("gate_m", 4))
                    turn_outputs(4, ("s_new", 2 * NB))
                    pe.wait_ge(*at("gate_lo", 5))
                    for k in range(12, 20):
                        unit(k)

            def pooling(stage):
                at = marks.here(stage)
                pe.wait_ge(*at("x_n", 0))
                for c in range(DC):
                    mm = turn(ps[0:HIST + NB, 4 + c // 4, (c % 4) * P:(c % 4 + 1) * P], x[:, c, SEQ - HIST:T], P)
                    if c % 4 == 3:
                        mm.then_inc(S["pl_tail"], 1)
                pe.wait_ge(*at("pl_in", 48))
                n = NB * HIST
                for c in range(DC):
                    mm = turn(ps[:, 6 + c // 4, (c % 4) * n:(c % 4 + 1) * n], hist[0:n, c * P:(c + 1) * P], n)
                    if c % 4 == 3:
                        mm.then_inc(S["pl_hist"], 1)
                for g in range(4):
                    pe.wait_ge(*unit_mark("w_lo", stage, 0, g))
                    pe.wait_ge(*at("d_lo", g + 1))
                    pe.wait_ge(*(at("y_sc", 2 * g) if g else at("z_add", 0)))
                    slot = slot_of(stage, g) % 2
                    wh, wl = (w[:, slot, 0:512].rearrange("p (c n) -> p c n", c=2) for w in (w_h, w_l))
                    for m in range(2):
                        for b, cols in enumerate(prompt_halves()):
                            for c in range(2):
                                to = slice(m * P, (m + 1) * P)
                                mm = three(ps[:, 2 * m + b, 0:HALF], wh[:, c, to], wl[:, c, to],
                                           d_h[:, 2 * g + c, cols], d_l[:, 2 * g + c, cols], c == 0, c == 1)
                    mm.then_inc(S["mm"], 1)

            def rotate(at, k, m, slot):
                for b, cols in enumerate(prompt_halves()):
                    mm = M.matmul(ps[:, 4 + b, 0:HALF], m, d_raw[:, slot, cols], start=True, stop=True)
                mm.then_inc(S["rot"], 1)

            def index(stage):
                at = marks.here(stage)
                pe.wait_ge(*at("z_add", 0))
                multiply_first(pe, stage, x_h, x_l)
                pe.wait_ge(*at("tab_in", 80))
                for k in range(4):
                    if k >= 2:
                        pe.wait_ge(*at("d_raw", k - 1))
                        multiply(pe, stage, 0, k, x_h, x_l, DC)
                    if k < 3:
                        pe.wait_ge(*at("d_raw", k + 1))
                        if k:
                            pe.wait_ge(*at("d_rope", 3 * k))
                        rotate(at, k, roti, k % 2)
                pe.wait_ge(*at("d_rope", 9))
                pe.wait_ge(*at("d_raw", 4))
                for t in range(QT):
                    turn(ps[:, 6, t * P:(t + 1) * P], d_raw[:, 1, t * P:(t + 1) * P], P)
                    turn(ps[:, 7, P + t * ID:P + (t + 1) * ID], d_f[0:ID, 0, t * P:(t + 1) * P], ID)
                turn(ps[0:NB, 7, 0:P], d_raw[:, 1, SEQ:T], P)
                turn(ps[0:NB, 7, 384:448], d_f[0:ID, 0, SEQ:T], ID).then_inc(S["wi_tp"], 1)
                pe.wait_ge(*at("d_lo", 3))
                for n in range(12):
                    t, h = n // 4 + 1, n % 4
                    rows, tile = slice(ID * (h % 2), ID * (h % 2) + ID), slice(t * P, (t + 1) * P)
                    w = (t + 1) * P
                    pe.wait_ge(*(at("rl", n - 3) if n >= 4 else at("ki_cp", 4)))
                    three(ps[:, 4 + n % 4, 0:w], qi_h[rows, h // 2, tile], qi_l[rows, h // 2, tile], ki_h[rows, 0:w],
                          ki_l[rows, 0:w]).then_inc(S["s_idx"], 1)

            def queries(stage):
                at = marks.here(stage)
                pe.wait_ge(*at("rl", 0))
                for k in range(8):
                    pe.wait_ge(*at("d_raw", k - 1))
                    multiply(pe, stage, 0, k, x_h, x_l, DC)
                    pe.wait_ge(*at("d_raw", k + 1))
                    pe.wait_ge(*at("d_rope", 3 * k))
                    rotate(at, k, rotm, k % 2)

            def attend(stage, n):
                pieces = [(0, range(0, 4)), (0, range(4, 8)), (1, range(0, 2)), (1, range(2, 4))]
                pe.wait_ge(*marks.here(stage)("d_raw", 0))
                for k, part in pieces:
                    multiply(pe, stage, 0, k, x_h, x_l, DC, part)
                for i in passes(pe, n):
                    at = marks.here(stage, i)
                    for q in range(2):
                        pe.wait_ge(*at("d_raw", 2 * q + 1))
                        pe.wait_ge(*at("o_lo", q))
                        rotate(at, q, rotm, 0)
                        multiply(pe, stage, i, 2 * q + 1, x_h, x_l, DC, range(4, 8))
                        pe.wait_ge(*at("d_rope", 3 * q + 3))
                        pe.wait_ge(*at("p_lo", 4 * q))
                        for t in range(QT):
                            turn(ps[:, 6, t * P:(t + 1) * P], d_f[:, 0, t * P:(t + 1) * P], P)
                        turn(ps[0:NB, 4, 0:P], d_f[:, 0, SEQ:T], P).then_inc(S["kk_tp"], 1)
                        pe.wait_ge(*at("d_raw", 2 * q + 2))
                        for t in range(QT):
                            turn(ps[:, 7, t * P:(t + 1) * P], d_raw[:, 1, t * P:(t + 1) * P], P)
                        turn(ps[0:NB, 5, 0:P], d_raw[:, 1, SEQ:T], P).then_inc(S["vv_tp"], 1)
                        pe.wait_ge(*at("qa_l", q + 1))
                        pe.wait_ge(*at("k_lo", q + 1))
                        for t in range(QT):
                            w, tile = (t + 1) * P, slice(t * P, (t + 1) * P)
                            if t == 0:
                                pe.wait_ge(*at("kn_cp", 2 * q + 2))
                            elif t == 1:
                                pe.wait_ge(*at("vn_cp", 2 * q + 2))
                            elif t == 3:
                                pe.wait_ge(*at("vv_lo", q + 1))
                            three(ps[:, 4 + t, 0:w], qa_h[:, tile], qa_l[:, tile], ka_h[:, 0:w], ka_l[:, 0:w]
                                  ).then_inc(S["s_mm"], 1)
                        for t in range(QT):
                            m = 4 * q + t
                            if q == 0:
                                multiply(pe, stage, i, 2 + pieces[t][0], x_h, x_l, DC, pieces[t][1])
                            elif not isinstance(i, int):
                                multiply(pe, stage, i + 1, pieces[t][0], x_h, x_l, DC, pieces[t][1])
                            pe.wait_ge(*at("p_n", m + 1))
                            for j in range(t + 1):
                                mm = turn(ps[:, 4 + t, j * P:(j + 1) * P], pe_[:, t % 2, j * P:(j + 1) * P], P)
                            mm.then_inc(S["p_tp"], 1)
                            if t:
                                output(at, m - 1, t - 1)
                        output(at, 4 * q + 3, 3).then_inc(S["pv"], 1)

            def output(at, m, t):
                pe.wait_ge(*at("p_lo", m + 1))
                for j in range(t + 1):
                    mm = three(ps[:, 4, t * P:(t + 1) * P], va_h[:, j], va_l[:, j], p_h[:, t % 2, j * P:(j + 1) * P],
                               p_l[:, t % 2, j * P:(j + 1) * P], j == 0, j == t)
                return mm

            def past(stage):
                at = marks.here(stage)
                pe.wait_ge(*at("sv_i", 0))

                def spread_q(b):
                    if b >= 2:
                        pe.wait_ge(*at("kmm", 4 * b - 4))
                    for h in range(AH):
                        mm = M.matmul(ps[:, 2 * (b % 2) + h // 4, (h % 4) * AD:(h % 4 + 1) * AD],
                                      qs_d[:, h, b:b + 1].to_broadcast([P, P]), ident[:], start=True, stop=True)
                    mm.then_inc(S["qc"], 1)

                spread_q(0)
                spread_q(1)
                pe.wait_ge(*at("pt_in", 48))
                for c in range(2):
                    mm = turn(ps[0:NB, 7, c * P:(c + 1) * P], qi_d[:, c, :], P)
                mm.then_inc(S["qi_t"], 1)
                pe.wait_ge(*at("qi_c", 1))
                for h in range(IH):
                    mm = turn(ps[0:ID, 7, 256 + h * NB:256 + (h + 1) * NB], qiS[:, h * ID:(h + 1) * ID], NB)
                mm.then_inc(S["qi_t"], 1)
                pe.wait_ge(*at("prodi", 1))
                pe.wait_ge(*at("qm", 13))
                M.matmul(ps[0:32, 7, 300:301], prodi[0:ID].rearrange("p h b -> p (h b)"), avg[0:ID, 0:1], start=True, stop=True)
                M.matmul(ps[0:32, 7, 301:302], wd[0:NB].rearrange("p h b -> p (h b)"), avg[0:NB, 0:1], start=True,
                         stop=True).then_inc(S["ki_w"], 1)
                pe.wait_ge(*at("kx_in", 512))
                for b in range(NB):
                    if b >= 2:
                        pe.wait_ge(*at("kx_c", b - 1))
                    for j in range(PAGES):
                        mm = turn(ps[0:ID, 4 + b % 2, j * P:(j + 1) * P], kix[:, b * PAGES + j, :], P)
                    mm.then_inc(S["kx_t"], 1)
                    pe.wait_ge(*at("kx_c", b + 1))
                    mm = M.matmul(ps[0:32, 6, :], qm[0:ID, b].rearrange("p h b -> p (h b)"), kiT[0:ID, b % 2], start=(b == 0),
                                  stop=(b == NB - 1))
                mm.then_inc(S["kx_mm"], 1)
                pe.wait_ge(*at("rel", 2))
                pe.wait_ge(*at("lw", 1))
                M.matmul(ps[0:NB, 5, :], lw, rel[:, 0:PAST], start=True, stop=True)
                M.matmul(ps[0:NB, 7, 302:303], lw, rel[:, PAST:PAST + 1], start=True, stop=True).then_inc(S["sc_mm"], 1)
                pe.wait_ge(*at("sp_pick", 33))
                M.matmul(ps[0:64, 4, :], expand, scs[:, 0:PAST], start=True, stop=True)
                M.matmul(ps[0:64, 7, 303:304], expand, scs[:, PAST:PAST + 1], start=True, stop=True).then_inc(S["b64_mm"], 1)
                pe.wait_ge(*at("b64", 2))

                for b in range(2, NB):
                    spread_q(b)
                pe.wait_ge(*at("kr_v", NB * 2))
                pe.wait_ge(*at("kr_a", NB * 2))
                pe.wait_ge(*at("pr", 1))
                M.matmul(ps[0:64, 7, 0:1], prod, avg[:, 0:1], start=True, stop=True)
                for j in range(PAGES):
                    mm = turn(ps[0:64, 6, j * P:(j + 1) * P], sp_[:, j, :], P)
                mm.then_inc(S["s64"], 1)
                pe.wait_ge(*at("dg", 1))
                for j in range(PAGES):
                    turn(ps[:, 6, j * 64:(j + 1) * 64], sm[:, j * P:(j + 1) * P], 64)
                M.matmul(ps[:, 7, 64:128], avg[0:64, :], dg, start=True, stop=True).then_inc(S["pt_t"], 1)
                for b in range(NB):
                    pe.wait_ge(*at("pc", b + 1))
                    pe.wait_ge(*at(f"kp_in{b % 2}", 64 * (b // 2 + 5)))
                    for j in range(PAGES):
                        for a in range(2):
                            mm = M.matmul(ps[0:64, 4 + a, :], pz[:, j, b, :], kvp[:, b % 2, j, a * SEQ:(a + 1) * SEQ],
                                          start=(b + j == 0), stop=(b == NB - 1 and j == PAGES - 1))
                    mm.then_inc(S["ov"], 1)
                pe.wait_ge(*at("om", 1))
                for h in range(AH):
                    mm = M.matmul(ps[:, 6, h * NB:(h + 1) * NB], om[:, h * AD:(h + 1) * AD], pick_b, start=True, stop=True)
                mm.then_inc(S["oh"], 1)

            def project(stage):
                at = marks.here(stage)
                pe.wait_ge(*at("o_lo", 0))
                for k in range(8):
                    pe.wait_ge(*(at("d_raw", 0) if k < 2 else at("z_add", k - 1)))
                    multiply(pe, stage, 0, k, o_h, o_l, DC)

            def up(stage, n):
                after_norm = n == FA // 2
                for i in passes(pe, n, int(after_norm)):
                    at = marks.here(stage, i)
                    if after_norm and isinstance(i, int) and i == 0:
                        multiply_first(pe, stage, x_h, x_l)
                    for k in range(2 if after_norm and isinstance(i, int) and i == 0 else 0, 4):
                        pe.wait_ge(*at(("sil", "h_raw")[k % 2], k // 2))
                        multiply(pe, stage, i, k, x_h, x_l, DC)

            def down(stage, cs):
                at = marks.here(stage)
                pe.wait_ge(*at("h_lo", 0))
                for k in range(8):
                    pe.wait_ge(*(at(("sil", "h_raw")[k], 0) if k < 2 else at("z_add", k - 1)))
                    multiply(pe, stage, 0, k, h_h, h_l, cs)

            def norm(stage, before):
                at = marks.here(stage)
                for n, (total, name) in enumerate(((sum_s, "sum_s"), (sum_q, "sum_q"))):
                    pe.wait_ge(*at(name, 0))
                    for b, cols in enumerate(prompt_halves()):
                        M.matmul(ps[:, 4 + 2 * n + b, 0:HALF], avg[:], total[:, cols], start=True, stop=True
                                 ).then_inc(S["stat"], 1)

            pe.wait_ge(S["tiny_c"], 2)
            for stage, n, units in STAGES:
                kind = kind_of(stage)
                if kind == "start":
                    start(stage)
                elif kind == "ret":
                    ret(stage)
                elif kind == "pool":
                    pooling(stage)
                elif kind == "idx":
                    index(stage)
                elif kind == "q":
                    queries(stage)
                elif kind == "kv":
                    attend(stage, n)
                elif kind == "past":
                    past(stage)
                elif kind == "proj":
                    project(stage)
                elif kind in ("up_a", "up_b"):
                    up(stage, n)
                elif kind == "down_a":
                    down(stage, FA)
                elif kind == "down_b":
                    down(stage, FB)
                elif kind == "norm":
                    norm(stage, None)
                elif kind == "end":
                    at = marks.here(stage)
                    pe.wait_ge(*at("x_n", 0))
                    for c in range(DC):
                        if c >= 2:
                            pe.wait_ge(*at("y_cp", 2 * c - 2))
                        for t in range(QT):
                            mm = turn(ps[:, 4 + c % 2, t * P:(t + 1) * P], x[:, c, t * P:(t + 1) * P], P)
                        mm.then_inc(S["y_tp"], 1)
                        turn(ps[0:NB, 6 + c % 2, 0:P], x[:, c, SEQ:T], P).then_inc(S["ys_tp"], 1)


def constants():
    f = np.float32
    pos = np.concatenate([np.arange(SEQ), np.full(NB, PAST)]).astype(f)

    def table(half, rows):
        inv = np.power(f(10000.0), -np.arange(half, dtype=f) / f(half)).astype(f)
        ang = (pos[None, :] * inv[np.arange(rows) % half][:, None]).astype(f)
        return np.stack([np.cos(ang), np.sin(ang)]).astype(f)

    lg = np.log1p(-np.exp2(-5.0 - np.arange(RH, dtype=np.float64)))
    n, j = np.arange(SEQ), np.arange(P)
    diff = n[None, :] - j[:, None]
    decay = np.where(diff[None] >= 0, np.exp(np.maximum(diff, 0)[None] * lg[:, None, None]), 0.0).astype(f)
    col = np.zeros((RH, P, 8), f)
    for t in range(QT):
        col[:, :, t] = np.exp((SEQ - 1.0 - (t * P + j))[None, :] * lg[:, None])
    col[:, :, 4] = np.exp(lg)[:, None]
    def exchange(width):
        m = np.zeros((P, P), f)
        for r in range(P):
            h = r % width
            m[r + width // 2 if h < width // 2 else r - width // 2, r] = -1.0 if h < width // 2 else 1.0
        return m

    inv = np.concatenate([1.0 / np.minimum(w, np.arange(16) + 1) for w in WINDOWS]).astype(f)
    return {"dsa_tab": table(AD // 2, P), "idx_tab": table(ID // 2, P), "dsa_rot": exchange(AD), "idx_rot": exchange(ID),
            "causal": np.where(j[None, :] <= j[:, None], 0.0, -BIG).astype(f), "inv_count": np.tile(inv, (P, 1)),
            "fold": np.tile(np.eye(NB, dtype=f), (IH, 1)), "expand": np.repeat(np.eye(NB, dtype=f), AH, axis=1),
            "picks": np.hstack([np.tile(np.eye(AH, dtype=f), (NB, 1)), np.repeat(np.eye(NB, dtype=f), AH, axis=0)]),
            "ident": np.eye(P, dtype=f), "ret_tab": table(P, P), "decay": decay, "head_col": col}


_INS = ["x_prompt", "x_sample", "state_ret", "state_pool", "cache_k", "cache_v", "cache_kidx", "page_table",
        "ret_w_in", "ret_norm_g", "ret_w_out", "pool_w_grp", "pool_scale", "dsa_w_in", "dsa_w_out",
        "ffn_w_in", "ffn_w_out", "ln_g", "ln_b"]
_OUTS = [(1, SEQ, D), (NB, 1, D), (2, 1, RH, RK, RV), (2, NB, RH, RK, RV), (1, 1, HIST, D), (1, NB, HIST, D),
         (1, 1, SEQ, AH, AD), (1, 1, SEQ, AH, AD), (1, 1, SEQ, ID), (1, NB, 1, AH, AD), (1, NB, 1, AH, AD),
         (1, NB, 1, ID)]


def kernel(**inputs):
    import concourse.bacc as bacc
    from concourse.bass_utils import run_bass_kernel_spmd as run

    nc = bacc.Bacc("TRN2", target_bir_lowering=False, num_devices=1)
    arrays = {name: np.ascontiguousarray(inputs[name]) for name in _INS}
    arrays.update(constants())
    ins = {name: nc.dram_tensor(f"in_{name}", a.shape, mybir.dt.from_np(a.dtype), kind="ExternalInput").ap()
           for name, a in arrays.items()}
    outs = [nc.dram_tensor(f"out_{i}", shape, F32, kind="ExternalOutput").ap() for i, shape in enumerate(_OUTS)]
    trunk(nc, ins, outs)
    r = run(nc, [{f"in_{name}": a for name, a in arrays.items()}], core_ids=[0])
    return tuple(r.results[0][f"out_{i}"] for i in range(len(_OUTS)))
```
